# Optimizing a Trainium2 kernel written in Bass

```python
import jax, jax.numpy as jnp
from jax import lax
import numpy as np
import math

D_MODEL = 2048
BATCH = 1
SEQ = 256
DEPTH = 1

CTX_LEN = 256
GRID_W = 64
A_HEADS = 8
A_DK = 128
A_DV = 128
A_WIDTH = A_HEADS * A_DK
B_WIDTH = 1024
CONV_W = 3
D_FF = 5632
CHUNK = 64
EPS = 1e-6
REC_COLS = 4 * A_WIDTH
IN_COLS = REC_COLS + A_WIDTH + 3 * B_WIDTH + 2 * D_MODEL


def rms_norm(x, g):
    x32 = x.astype(jnp.float32)
    y = x32 * lax.rsqrt(jnp.mean(x32 * x32, axis=-1, keepdims=True) + EPS)
    return (y * g.astype(jnp.float32)).astype(x.dtype)

def modulate(h, shift, scale):
    return h * (1 + scale) + shift

def short_conv_1d(u, w):
    up = jnp.pad(u, ((0, 0), (1, 1), (0, 0)))
    return w[0] * up[:, :-2] + w[1] * up[:, 1:-1] + w[2] * up[:, 2:]

def dwconv_grid(u, w, bias):
    bn, L, F = u.shape
    rows = L // GRID_W
    u4 = u.reshape(bn, rows, GRID_W, F)
    y = lax.conv_general_dilated(u4, w[:, :, None, :].astype(u.dtype), (1, 1), 'SAME',
                                 dimension_numbers=('NHWC', 'HWIO', 'NHWC'), feature_group_count=F)
    return y.reshape(bn, L, F) + bias

def hgrn2_chunk_scan(q, k, v, logf, s0):
    bn, L, H, _ = q.shape
    nc = L // CHUNK

    def to_chunks(t):
        return jnp.moveaxis(t.reshape(bn, nc, CHUNK, H, t.shape[-1]), 1, 0)

    causal = jnp.tril(jnp.ones((CHUNK, CHUNK), dtype=bool))[None, :, :, None, None]

    def step(S, inp):
        qc, kc, vc, gc = inp
        b = jnp.cumsum(gc, axis=1)
        o_inter = jnp.einsum('bchk,bhkv->bchv', qc * jnp.exp(b), S)
        decay = jnp.exp(jnp.where(causal, b[:, :, None] - b[:, None, :], -jnp.inf))
        scores = jnp.einsum('bthk,bshk,btshk->btsh', qc, kc, decay)
        o_intra = jnp.einsum('btsh,bshv->bthv', scores, vc)
        b_last = b[:, -1]
        k_dec = kc * jnp.exp(b_last[:, None] - b)
        S = jnp.exp(b_last)[..., None] * S + jnp.einsum('bshk,bshv->bhkv', k_dec, vc)
        return S, o_inter + o_intra

    s_fin, o = lax.scan(step, s0, (to_chunks(q), to_chunks(k), to_chunks(v), to_chunks(logf)))
    o = jnp.moveaxis(o, 0, 1).reshape(bn, L, H, v.shape[-1])
    return o, s_fin

def token_mixer(h, w_in, lb_f, lb_b, a_norm_g, sconv_w, w_pa, w_pb, w_o, s0_f, s0_b, need_output):
    bn, L, _ = h.shape
    heads = lambda t: t.reshape(bn, L, A_HEADS, -1)
    z_rec = h @ w_in[:, :REC_COLS]
    q, zf, zb, v = jnp.split(z_rec, 4, axis=-1)
    q = heads(jax.nn.silu(q.astype(jnp.float32)))
    v = heads(v.astype(jnp.float32))

    def direction(zg, lb, s0, flip):
        f = lb + (1 - lb) * jax.nn.sigmoid(zg.astype(jnp.float32))
        qq, kk, vv, lf = q, heads(1 - f), v, heads(jnp.log(f))
        if flip:
            qq, kk, vv, lf = (jnp.flip(t, axis=1) for t in (qq, kk, vv, lf))
        o, s = hgrn2_chunk_scan(qq, kk, vv, lf, s0)
        return (jnp.flip(o, axis=1) if flip else o), s

    o_f, s_f = direction(zf, lb_f, s0_f, False)
    o_b, s_b = direction(zb, lb_b, s0_b, True)
    if not need_output:
        return None, s_f, s_b

    z_rest = h @ w_in[:, REC_COLS:]
    g, sb, sc, sh, ga, gb = jnp.split(
        z_rest, np.cumsum([A_WIDTH, B_WIDTH, B_WIDTH, B_WIDTH, D_MODEL])[:].tolist(), axis=-1)
    o = o_f + o_b
    o = o * lax.rsqrt(jnp.mean(o * o, axis=-1, keepdims=True) + EPS) * a_norm_g.astype(jnp.float32)
    y_a = (o.reshape(bn, L, A_WIDTH) * jax.nn.silu(g.astype(jnp.float32))).astype(h.dtype)
    y_b = sb * short_conv_1d(sc * sh, sconv_w)
    merged = jax.nn.sigmoid(ga) * (y_a @ w_pa) + jax.nn.sigmoid(gb) * (y_b @ w_pb)
    return merged @ w_o, s_f, s_b

def conv_ffn(h, w_up, dw, db, w_down, on_grid):
    a, b = jnp.split(h @ w_up, 2, axis=-1)
    a = dwconv_grid(a, dw, db) if on_grid else short_conv_1d(a, dw[1]) + db
    return (jax.nn.silu(a) * b) @ w_down

def first_inputs(seed: int = 0) -> dict:
    key = jax.random.key(seed)
    ks = jax.random.split(key, 20)
    nrm = lambda k, shape, s: jax.random.normal(k, shape, jnp.float32) * s
    D = D_MODEL
    return {
        "x": nrm(ks[0], (BATCH, SEQ, D), 1.0),
        "c": nrm(ks[1], (BATCH, D), 1.0),
        "ctx": nrm(ks[2], (BATCH, CTX_LEN, D), 1.0),
        "c_ctx": nrm(ks[3], (D,), 1.0),
        "w_mod": nrm(ks[4], (DEPTH, D, 6 * D), 0.5 * D ** -0.5),
        "b_mod": nrm(ks[5], (DEPTH, 6 * D), 0.02),
        "norm1_g": 1.0 + nrm(ks[6], (DEPTH, D), 0.02),
        "w_in": nrm(ks[7], (DEPTH, D, IN_COLS), D ** -0.5),
        "lb_raw": nrm(ks[8], (DEPTH + 1, 2, A_WIDTH), 0.5),
        "a_norm_g": 1.0 + nrm(ks[9], (DEPTH, A_DV), 0.02),
        "sconv_w": nrm(ks[10], (DEPTH, CONV_W, B_WIDTH), CONV_W ** -0.5),
        "w_pa": nrm(ks[11], (DEPTH, A_WIDTH, D), A_WIDTH ** -0.5),
        "w_pb": nrm(ks[12], (DEPTH, B_WIDTH, D), B_WIDTH ** -0.5),
        "w_o": nrm(ks[13], (DEPTH, D, D), D ** -0.5),
        "norm2_g": 1.0 + nrm(ks[14], (DEPTH, D), 0.02),
        "w_up": nrm(ks[15], (DEPTH, D, 2 * D_FF), D ** -0.5),
        "ffn_dw": nrm(ks[16], (DEPTH, 3, 3, D_FF), 1.0 / 3.0),
        "ffn_db": nrm(ks[17], (DEPTH, D_FF), 0.02),
        "w_down": nrm(ks[18], (DEPTH, D_FF, D), D_FF ** -0.5),
        "final_g": 1.0 + nrm(ks[19], (D,), 0.02),
    }

def first_block(x, c, ctx, c_ctx, w_mod, b_mod, norm1_g, w_in, lb_raw, a_norm_g, sconv_w,
              w_pa, w_pb, w_o, norm2_g, w_up, ffn_dw, ffn_db, w_down, final_g):
    bn = x.shape[0]
    D = D_MODEL
    lbs = jnp.cumsum(jax.nn.softmax(lb_raw.astype(jnp.float32), axis=0), axis=0)
    zero_state = jnp.zeros((bn, A_HEADS, A_DK, A_DV), jnp.float32)
    silu_c = jax.nn.silu(c)
    silu_cc = jax.nn.silu(c_ctx)
    h_ctx = ctx
    for l in range(DEPTH):
        last = l == DEPTH - 1
        mod = silu_c @ w_mod[l] + b_mod[l]
        sh1, sc1, g1, sh2, sc2, g2 = (t[:, None, :] for t in jnp.split(mod, 6, axis=-1))
        n_ctx_mod = 2 if last else 6
        mod_c = silu_cc @ w_mod[l][:, :n_ctx_mod * D] + b_mod[l][:n_ctx_mod * D]
        mc = jnp.split(mod_c, n_ctx_mod)
        mix_args = (w_in[l], lbs[l, 0], lbs[l, 1], a_norm_g[l], sconv_w[l], w_pa[l], w_pb[l], w_o[l])
        hc = modulate(rms_norm(h_ctx, norm1_g[l]), mc[0], mc[1])
        out_c, s_f, s_b = token_mixer(hc, *mix_args, zero_state, zero_state, not last)
        hx = modulate(rms_norm(x, norm1_g[l]), sh1, sc1)
        out_x, _, _ = token_mixer(hx, *mix_args, s_f, s_b, True)
        x = x + g1 * out_x
        x = x + g2 * conv_ffn(modulate(rms_norm(x, norm2_g[l]), sh2, sc2),
                              w_up[l], ffn_dw[l], ffn_db[l], w_down[l], True)
        if not last:
            h_ctx = h_ctx + mc[2] * out_c
            h_ctx = h_ctx + mc[5] * conv_ffn(modulate(rms_norm(h_ctx, norm2_g[l]), mc[3], mc[4]),
                                             w_up[l], ffn_dw[l], ffn_db[l], w_down[l], False)
    return rms_norm(x, final_g)


N_META = 16
BLOCK_Q = 128
SB_HEADS = 8
SB_HEAD_DIM = 128
SB_WIDTH = SB_HEADS * SB_HEAD_DIM
DIFF_HEADS = 8
DIFF_QK_DIM = 64
DIFF_V_DIM = 2 * DIFF_QK_DIM
DIFF_QK_WIDTH = DIFF_HEADS * 2 * DIFF_QK_DIM
DIFF_WIDTH = DIFF_HEADS * DIFF_V_DIM
MIX_WIDTH = SB_WIDTH + DIFF_WIDTH
IN_SIZES = (SB_WIDTH, SB_WIDTH, SB_WIDTH, SB_WIDTH,
            DIFF_QK_WIDTH, DIFF_QK_WIDTH, DIFF_WIDTH, DIFF_WIDTH)
IN_WIDTH = 4 * SB_WIDTH + 2 * DIFF_QK_WIDTH + 2 * DIFF_WIDTH
ROPE_THETA = 500000.0
ROT_DIM = DIFF_QK_DIM // 4
RMS_EPS = 1e-6
SUBLN_EPS = 1e-5


def rms_norm_2(x, w, eps=RMS_EPS):
    xf = x.astype(jnp.float32)
    y = xf * lax.rsqrt(jnp.mean(xf * xf, axis=-1, keepdims=True) + eps)
    return (y * w.astype(jnp.float32)).astype(x.dtype)

def lambda_init_for(layer):
    return 0.8 - 0.6 * math.exp(-0.3 * layer)

def partial_rope(x, cos, sin):
    half = ROT_DIM // 2
    c = cos[None, :, None, None, :]
    s = sin[None, :, None, None, :]
    x1 = x[..., :half]
    x2 = x[..., half:ROT_DIM]
    return jnp.concatenate([x1 * c - x2 * s, x2 * c + x1 * s, x[..., ROT_DIM:]], axis=-1)

def stick_breaking_block(q, k, v, q_pos, k_pos):
    z = jnp.einsum('bhqd,bhkd->bhqk', q, k) / math.sqrt(q.shape[-1])
    mask = k_pos[None, :] < q_pos[:, None]
    log_beta = jax.nn.log_sigmoid(z)
    log_keep = jnp.where(mask, jax.nn.log_sigmoid(-z), 0.0)
    tail = lax.cumsum(log_keep, axis=3, reverse=True) - log_keep
    a = jnp.where(mask, jnp.exp(log_beta + tail), 0.0)
    return jnp.einsum('bhqk,bhkd->bhqd', a, v)

def diff_attention_block(q, k, v, lam, q_pos, k_pos):
    s = jnp.einsum('bhcqd,bhckd->bhcqk', q, k) / math.sqrt(q.shape[-1])
    mask = k_pos[None, :] <= q_pos[:, None]
    p = jax.nn.softmax(jnp.where(mask, s, -jnp.inf), axis=-1)
    w = p[:, :, 0] - lam * p[:, :, 1]
    return jnp.einsum('bhqk,bhkd->bhqd', w, v)

def second_inputs(seed: int = 0) -> dict:
    key = jax.random.key(seed)
    ks = jax.random.split(key, 13)
    f32 = jnp.float32
    x = jax.random.normal(ks[0], (BATCH, SEQ, D_MODEL), f32)
    meta = jax.random.normal(ks[1], (N_META, D_MODEL), f32)
    norm_w = 1.0 + 0.02 * jax.random.normal(ks[2], (DEPTH, D_MODEL), f32)
    w_in = jax.random.normal(ks[3], (DEPTH, D_MODEL, IN_WIDTH), f32) * D_MODEL ** -0.5
    q_norm_w = 1.0 + 0.02 * jax.random.normal(ks[4], (DEPTH, DIFF_QK_DIM), f32)
    k_norm_w = 1.0 + 0.02 * jax.random.normal(ks[5], (DEPTH, DIFF_QK_DIM), f32)
    lambda_q1 = 0.1 * jax.random.normal(ks[6], (DEPTH, DIFF_QK_DIM), f32)
    lambda_k1 = 0.1 * jax.random.normal(ks[7], (DEPTH, DIFF_QK_DIM), f32)
    lambda_q2 = 0.1 * jax.random.normal(ks[8], (DEPTH, DIFF_QK_DIM), f32)
    lambda_k2 = 0.1 * jax.random.normal(ks[9], (DEPTH, DIFF_QK_DIM), f32)
    subln_w = 1.0 + 0.02 * jax.random.normal(ks[10], (DEPTH, DIFF_V_DIM), f32)
    w_out = jax.random.normal(ks[11], (DEPTH, MIX_WIDTH, D_MODEL), f32) * MIX_WIDTH ** -0.5
    return {"x": x, "meta": meta, "norm_w": norm_w, "w_in": w_in,
            "q_norm_w": q_norm_w, "k_norm_w": k_norm_w,
            "lambda_q1": lambda_q1, "lambda_k1": lambda_k1,
            "lambda_q2": lambda_q2, "lambda_k2": lambda_k2,
            "subln_w": subln_w, "w_out": w_out}

def second_block(x, meta, norm_w, w_in, q_norm_w, k_norm_w, lambda_q1, lambda_k1,
              lambda_q2, lambda_k2, subln_w, w_out):
    f32 = jnp.float32
    b, seq = x.shape[0], x.shape[1]
    h = jnp.concatenate(
        [jnp.broadcast_to(meta[None].astype(x.dtype), (b, N_META, D_MODEL)), x], axis=1)
    t_all = h.shape[1]
    pos = jnp.arange(t_all, dtype=f32)
    inv_freq = ROPE_THETA ** (-jnp.arange(0, ROT_DIM, 2, dtype=f32) / ROT_DIM)
    ang = pos[:, None] * inv_freq[None, :]
    cos, sin = jnp.cos(ang), jnp.sin(ang)
    split_at = list(np.cumsum(IN_SIZES)[:-1])
    real_blocks = [(N_META + i * BLOCK_Q, N_META + (i + 1) * BLOCK_Q)
                   for i in range(seq // BLOCK_Q)]

    for l in range(DEPTH):
        last = l == DEPTH - 1
        q_start = N_META if last else 0
        blocks = ([] if last else [(0, N_META)]) + real_blocks
        lam_init = lambda_init_for(l)

        u = rms_norm_2(h, norm_w[l])
        proj = jnp.einsum('btd,de->bte', u, w_in[l])
        sb_q, sb_k, sb_v, sb_g, df_q, df_k, df_v, df_g = jnp.split(proj, split_at, axis=-1)

        def heads(t, n, d):
            return t.reshape(b, t.shape[1], n, d).transpose(0, 2, 1, 3).astype(f32)

        sbq = heads(sb_q[:, q_start:], SB_HEADS, SB_HEAD_DIM)
        sbk = heads(sb_k, SB_HEADS, SB_HEAD_DIM)
        sbv = heads(sb_v, SB_HEADS, SB_HEAD_DIM)

        dq = df_q.reshape(b, t_all, DIFF_HEADS, 2, DIFF_QK_DIM).astype(f32)
        dk = df_k.reshape(b, t_all, DIFF_HEADS, 2, DIFF_QK_DIM).astype(f32)
        dq = partial_rope(rms_norm_2(dq, q_norm_w[l]), cos, sin).transpose(0, 2, 3, 1, 4)
        dk = partial_rope(rms_norm_2(dk, k_norm_w[l]), cos, sin).transpose(0, 2, 3, 1, 4)
        dq = dq[:, :, :, q_start:]
        dv = heads(df_v, DIFF_HEADS, DIFF_V_DIM)
        lam = (jnp.exp(jnp.sum(lambda_q1[l].astype(f32) * lambda_k1[l].astype(f32)))
               - jnp.exp(jnp.sum(lambda_q2[l].astype(f32) * lambda_k2[l].astype(f32)))
               + lam_init)

        sb_outs, df_outs = [], []
        for (a, e) in blocks:
            q_pos = jnp.arange(a, e)
            k_pos = jnp.arange(e)
            qa, qe = a - q_start, e - q_start
            sb_outs.append(stick_breaking_block(
                sbq[:, :, qa:qe], sbk[:, :, :e], sbv[:, :, :e], q_pos, k_pos))
            df_outs.append(diff_attention_block(
                dq[:, :, :, qa:qe], dk[:, :, :, :e], dv[:, :, :e], lam, q_pos, k_pos))

        t_q = t_all - q_start
        sb_o = jnp.concatenate(sb_outs, axis=2).transpose(0, 2, 1, 3).reshape(b, t_q, SB_WIDTH)
        df_o = jnp.concatenate(df_outs, axis=2).transpose(0, 2, 1, 3)
        df_o = (rms_norm_2(df_o, subln_w[l], SUBLN_EPS) * (1.0 - lam_init)).reshape(b, t_q, DIFF_WIDTH)

        mixed = jnp.concatenate(
            [sb_o * jax.nn.silu(sb_g[:, q_start:].astype(f32)),
             df_o * jax.nn.silu(df_g[:, q_start:].astype(f32))], axis=-1).astype(h.dtype)
        y = jnp.einsum('bte,ed->btd', mixed, w_out[l])
        h = jnp.concatenate([h[:, :q_start], h[:, q_start:] + y], axis=1)

    return h[:, N_META:]


def setup_inputs(seed=0):
    out = dict(first_inputs(seed))
    for name, value in second_inputs(seed + 1).items():
        if name != "x":
            out[name + "_2"] = value
    return out


def reference(
    x, c, ctx, c_ctx, w_mod, b_mod, norm1_g, w_in, lb_raw, a_norm_g, sconv_w, w_pa, w_pb, w_o,
    norm2_g, w_up, ffn_dw, ffn_db, w_down, final_g, meta_2, norm_w_2, w_in_2, q_norm_w_2,
    k_norm_w_2, lambda_q1_2, lambda_k1_2, lambda_q2_2, lambda_k2_2, subln_w_2, w_out_2,
):
    x = first_block(
        x, c, ctx, c_ctx, w_mod, b_mod, norm1_g, w_in, lb_raw, a_norm_g, sconv_w, w_pa, w_pb,
        w_o, norm2_g, w_up, ffn_dw, ffn_db, w_down, final_g,
    )
    return second_block(
        x, meta_2, norm_w_2, w_in_2, q_norm_w_2, k_norm_w_2, lambda_q1_2, lambda_k1_2,
        lambda_q2_2, lambda_k2_2, subln_w_2, w_out_2,
    )


_drawn_inputs = setup_inputs


def setup_inputs(seed=0):
    import zlib

    import numpy as np

    out = dict(_drawn_inputs(seed))
    spreads = {}
    factors = {'ctx': 8.0,
     'c_ctx': 8.0,
     'norm1_g': 6.082,
     'lb_raw': 8.0,
     'a_norm_g': 8.0,
     'norm2_g': 8.0,
     'ffn_db': 8.0,
     'norm_w_2': 3.953,
     'q_norm_w_2': 8.0,
     'k_norm_w_2': 7.693,
     'lambda_q1_2': 4.045,
     'lambda_k1_2': 2.941,
     'subln_w_2': 8.0}
    for name, (base, spread) in spreads.items():
        noise = np.random.default_rng([zlib.crc32(name.encode()), seed]).standard_normal(out[name].shape)
        drawn = base * np.exp(spread * noise) if base else spread * noise
        out[name] = __import__('jax').numpy.asarray(drawn.astype(out[name].dtype))
    for name, factor in factors.items():
        out[name] = (out[name] * factor).astype(out[name].dtype)
    return out
```

```python
from contextlib import ExitStack

import numpy as np

import concourse.bass as bass
from concourse import mybir

F32 = mybir.dt.float32
F32R = mybir.dt.float32r
ACT = mybir.ActivationFunctionType
ALU = mybir.AluOpType
AX = mybir.AxisListType

P = 128
D = 2048
KD = D // P
T = 256
HEADS = 8
FF = 5632 // P
NMETA = 16
TA = T + NMETA
GRID = 64
EPS = 1e-6
SUBLN_EPS = 1e-5
LAM_INIT = 0.8 - 0.6
LEVELS = 8
TINY = 2.0 ** -64
NEG = -1e30
DT = 11
DH = 6

PHASES = [
    ("mod1", 8, "mmmm"),
    ("rec", 8, "ssss"),
    ("mix", 8, "smsmsmsm"),
    ("merge", 8, "sssmsssm"),
    ("out", 8, "smsm"),
    ("up", 22, "ssss"),
    ("down", 8, "ssssssss"),
    ("attn", 8, "ssssssss"),
    ("proj", 4, "ssss"),
]
UNIT0, SPLIT0 = {}, {}
_u = _s = 0
for _n, _it, _k in PHASES:
    UNIT0[_n], SPLIT0[_n] = _u, _s
    _u += _it * len(_k)
    _s += _it * _k.count("s")
ITERS = {n: it for n, it, _ in PHASES}
KINDS = {n: k for n, _, k in PHASES}

VCOLS = {}
_o = 0
for _n, _w in [("norm1", KD), ("norm2", KD), ("final", KD), ("norm_2", KD), ("bmod", 6 * KD), ("lb", 32),
               ("anorm", 1), ("sconv", 24), ("dw", 9 * FF), ("db", FF), ("qn", 1), ("kn", 1),
               ("subln", 1), ("c", 2 * KD), ("lam", 4)]:
    VCOLS[_n] = (_o, _w)
    _o += _w
NVEC = _o

CCOLS = {}
_o = 0
for _n, _w in [("ident", P), ("masks", 8 * P)]:
    CCOLS[_n] = (_o, _w)
    _o += _w
NC1 = _o
C2COLS = {}
_o = 0
for _n, _w in [("tri", P), ("rot", P), ("cos", TA), ("sin", TA), ("sbmask", 3 * P), ("dfmask", P + NMETA + TA),
               ("blk64", P)]:
    C2COLS[_n] = (_o, _w)
    _o += _w
NC2 = _o

CHAIN = {"v_mod1": 6, "v_rec": 6, "v_mix": 37, "v_merge": 2, "v_up": 18, "v_attn": 26, "a_mix": 3, "a_attn": 4}


class Chain:

    def __init__(self, eng, sem):
        self.eng, self.sem, self.base, self.n, self.start = eng, sem, 0, 0, 0

    def enter(self, i, per):
        self.per, self.n, self.start = per, 0, self.base + i * per

    def leave(self, iters, name):
        assert self.n == self.per, f"CHAIN {name} {self.n}"
        self.base += iters * self.per
        self.n, self.start = 0, self.base

    def link(self, ins):
        self.n += 1
        ins.then_inc(self.sem, 1)
        self.eng.wait_ge(self.sem, self.start + self.n)

    def mark(self, ins):
        self.n += 1
        ins.then_inc(self.sem, 1)

    def wait(self):
        self.eng.wait_ge(self.sem, self.start + self.n)

    def straight(self):
        self.base = self.base + self.n
        self.n, self.start = 0, self.base


def build(nc, xct, metat, vec, con1, con2, wts, wdown, park, outt):
    ctx = ExitStack()
    with ctx:
        base = 16512

        def at(name, kb, shape, dt=F32):
            return nc.alloc_sbuf_tensor_at(name, shape, dt, offset=base + int(kb * 1024))

        def sem(name):
            return ctx.enter_context(nc.semaphore(name))

        RAW = at("raw", 0, [P, 4, 16, P])
        HI = at("hi", 32, [P, 2, 16, P], F32R)
        LO = at("lo", 48, [P, 2, 16, P], F32R)
        HX = at("hx", 64, [P, 4, KD, T], F32R)
        YAB = at("yab", 96, [P, 4, HEADS, T], F32R)
        XC = at("xc", 128, [P, 2, KD, T])
        SQ1 = at("sq1", 160, [P, 2, 4, 2, T])
        RS1 = at("rs1", 176, [P, 2, T])
        N1 = at("n1", 178, [P, 2, T])
        HN1 = at("hn1", 180, [P, 2, T])
        FG = at("fg", 144, [P, 2, HEADS, T])
        VT = at("vt", 160, [P, 2, HEADS * P])
        ST = at("st", 168, [P, 2, HEADS, P])
        QF = at("qf", 176, [P, HEADS, T])
        MRG = at("mrg", 144, [P, 2, KD, T], F32R)
        X1 = at("x1", 128, [P, KD, T])
        SH = at("sh", 96, [P, FF, T], F32R)
        SL = at("sl", 140, [P, FF, T], F32R)
        XF = at("xf", 64, [P, KD, T])
        U2 = at("u2", 96, [P, 2, KD, TA], F32R)
        MIX = at("mix", 130, [P, 2, 2 * HEADS, T], F32R)
        CON2 = at("con2", 162, [P, NC2])
        CON1 = at("con1", 184 + 13.5, [P, NC1])
        cbase = 184 + 13.5 + NC1 / 256
        VEC = at("vec", cbase, [P, NVEC])
        MODV = at("modv", cbase + 2.75, [P, 6 * KD, 2])
        AM1 = at("am1", cbase + 3.5, [P, KD, 2])
        AM2 = at("am2", cbase + 3.625, [P, KD])
        LBV = at("lbv", cbase + 3.6875, [P, 3, 16])
        CS = at("cs", cbase + 3.875, [P, KD, 2])
        ONESR = at("onesr", cbase + 4.0, [P, P])
        SMALL = at("small", cbase + 4.5, [P, 32])
        SG = at("sg", 128, [P, 2, 2, T])
        FC = at("fc", 132, [P, 2, T])
        LC = at("lc", 134, [P, 2, T])
        EXC = at("exc", 136, [P, 2, T])
        KDT = at("kdt", 138, [P, 4, P])
        VS = at("vs", 140, [P, 2, T])
        VCT = at("vct", 142, [P, 2, P])
        SGQ = at("sgq", 143, [P, T])
        ONE = at("one", 184, [P, T])
        AR = at("ar", 128, [P, 4, T])
        TT0 = at("tt0", 132, [P, 3, T])
        QK1 = at("qk1", 135, [P, 2, T])
        QK0 = at("qk0", 137, [P, 2, T])
        QL = at("ql", 139, [P, 2, 2, T])
        KS = at("ks", 143, [P, T])
        TT1 = at("tt1", 184, [P, 3, P])
        SCT = at("sct", 185.5, [P, 2, 4, P])
        SC = at("sc", 189.5, [P, 2, T])
        QS = at("qs", 191.5, [P, 2, T])
        GS = at("gs", 193.5, [P, T])
        SGG = at("sgg", 194.5, [P, T])
        UP = at("up", 195.5, [P, T + 8])
        ON = at("on", 185.5, [P, 2, P])
        OSQ = at("osq", 186.5, [P, 2, P])
        YT = at("yt", 187.5, [P, T])
        SCB = at("scb", cbase + 4.625, [P, T])
        GA = at("ga", 184, [P, T])
        GB = at("gb", 185, [P, T])
        M1 = at("m1", 186, [P, T])
        M2 = at("m2", 187, [P, T])
        SQ2 = at("sq2", 184, [P, 2, T])
        ZERO = at("zero", 196.25, [P, T])
        RS2 = at("rs2", 187, [P, T])
        N2 = at("n2", 188, [P, 8, T])
        AT = at("at", 184, [P, T])
        CV = at("cv", 185, [P, T])
        SGU = at("sgu", 186, [P, T])
        S1 = at("s1", 187, [P, T])
        SQ3 = at("sq3", 184, [P, 2, T])
        METT = at("mett", 80, [P, KD, NMETA])
        RS3 = at("rs3", 81, [P, TA])
        SQ4 = at("sq4", 82.0625, [P, 2, TA])
        N3 = at("n3", 84.1875, [P, 4, TA])
        a0 = 80

        DQK = at("dqk", a0, [P, 2, TA])
        DN = at("dn", a0 + 2.125, [P, 2, TA])
        DR = at("dr", a0 + 4.25, [P, 2, TA])
        DV = at("dv", a0 + 6.375, [P, TA])
        DVT = at("dvt", a0 + 7.4375, [P, 3, P])
        SV = at("sv", a0 + 8.9375, [P, TA])
        SVT = at("svt", a0 + 10, [P, 3, P])
        SQF = at("sqf", a0 + 11.5, [P, T])
        SKF = at("skf", a0 + 12.5, [P, TA])
        GSB = at("gsb", a0 + 13.5625, [P, T])
        GDF = at("gdf", a0 + 14.5625, [P, T])
        b0 = 162 + NC2 / 256
        SS = at("ss", b0, [P, 2, P + NMETA + TA])
        WTS = at("wts", b0 + 3.25, [P, 3 * P])
        WTM = at("wtm", b0 + 4.75, [P, T])
        ZS = at("zs", b0 + 5.75, [P, 3 * P])
        ZM = at("zm", b0 + 7.25, [P, T])
        LZ = at("lz", b0 + 8.25, [P, 3 * P])
        LM = at("lm", b0 + 9.75, [P, T])
        AZ = at("az", b0 + 10.75, [P, 3 * P])
        AM = at("am", b0 + 12.25, [P, T])
        MT = at("mt", b0 + 13.25, [P, T])
        OD = at("od", b0 + 14.25, [P, T])
        RSD = at("rsd", b0 + 15.25, [P, T])
        SGA = at("sga", b0 + 16.25, [P, T])
        ONEP = at("onep", b0 + 17.25, [P, P])
        ON128 = at("on128", b0 + 17.75, [P, P])
        ATS = at("ats", b0 + 18.25, [P, 24])
        OUTS = at("outs", 80, [P, KD, T])

        ACC = ctx.enter_context(nc.psum_tensor("acc", [P, 4, 512], F32))
        AUX = ctx.enter_context(nc.psum_tensor("aux", [P, 4, 512], F32))

        raw_full = [sem(f"raw_full{i}") for i in range(4)]
        hi_half, lo_half = sem("hi_half"), sem("lo_half")
        mm_half = sem("mm_half")
        bank_free = sem("bank_free")
        v_chain, a_chain = sem("v_chain"), sem("a_chain")
        in_vec, in_con, in_x, in_con2, in_meta = (sem(n) for n in ("in_vec", "in_con", "in_x", "in_con2", "in_meta"))
        c_sig, c_silu, ones_set = sem("c_sig"), sem("c_silu"), sem("ones_set")
        lb_exp, lb_max = sem("lb_exp"), sem("lb_max")
        sq1_done, ss1_mm, rs1_done = sem("sq1_done"), sem("ss1_mm"), sem("rs1_done")
        n1_ready, h1_aff, hx_ready = sem("n1_ready"), sem("h1_aff"), sem("hx_ready")
        gate_sig = sem("gate_sig")
        ctx_f, ctx_ln, ctx_scan, ctx_exp, kd_ready = (sem(n) for n in ("ctx_f", "ctx_ln", "ctx_scan", "ctx_exp", "kd_ready"))
        kd_tr, kdt_ready, v_tr, vt_ready, s_mm, s_ready = (
            sem(n) for n in ("kd_tr", "kdt_ready", "v_tr", "vt_ready", "s_mm", "s_ready"))
        f_ready, f_ln, lv_sum, lv_exp, lv_mul, ks_ready = (
            sem(n) for n in ("f_ready", "f_ln", "lv_sum", "lv_exp", "lv_mul", "ks_ready"))
        sc_mm, sc_read, o_mm, o_rstd, on_ready, on_tr, ya_ready = (
            sem(n) for n in ("sc_mm", "sc_read", "o_mm", "o_rstd", "on_ready", "on_tr", "ya_ready"))
        yb_ready, mrg_ready = sem("yb_ready"), sem("mrg_ready")
        in_x1, x1_chunk, sq2_done, ss2_mm, rs2_done, n2_ready, h2_aff, hx2_ready, x1_out, zero_set = (
            sem(n) for n in ("in_x1", "x1_chunk", "sq2_done", "ss2_mm", "rs2_done", "n2_ready", "h2_aff",
                             "hx2_ready", "x1_out", "zero_set"))
        a_copied, cv_ready, cv_sig, s_hidden = sem("a_copied"), sem("cv_ready"), sem("cv_sig"), sem("s_hidden")
        in_x1b, x2_chunk, sq3_done, ss3_mm, rs3_done = (
            sem(n) for n in ("in_x1b", "x2_chunk", "sq3_done", "ss3_mm", "rs3_done"))
        xf_ready, sq4_done, ss4_mm, rs4_done, n3_ready, u2_ready = (
            sem(n) for n in ("xf_ready", "sq4_done", "ss4_mm", "rs4_done", "n3_ready", "u2_ready"))
        at_const, lam_mm, lam_exp, lam_ready, lam_prod = (
            sem(n) for n in ("at_const", "lam_mm", "lam_exp", "lam_ready", "lam_prod"))
        d_sq, d_ms, d_rstd, d_norm, d_rot, d_rope, dv_tr, dvt_ready = (
            sem(n) for n in ("d_sq", "d_ms", "d_rstd", "d_norm", "d_rot", "d_rope", "dv_tr", "dvt_ready"))
        d_sc, d_max, d_exp, d_w, d_wtr, d_wt, d_av, d_osq, d_oms, d_orstd = (
            sem(n) for n in ("d_sc", "d_max", "d_exp", "d_w", "d_wtr", "d_wt", "d_av", "d_osq", "d_oms", "d_orstd"))
        b_v, bv_tr, svt_ready, b_z, b_zs, b_ln, b_sp, b_tail, b_arg, b_a, b_av = (
            sem(n) for n in ("b_v", "bv_tr", "svt_ready", "b_z", "b_zs", "b_ln", "b_sp", "b_tail", "b_arg", "b_a", "b_av"))
        mix_ready = sem("mix_ready")
        out_done = sem("out_done")

        def vc(name, j=0, n=1):
            o = VCOLS[name][0] + j
            return VEC[:, o:o + n]

        def vcd(name, j):
            return VEC[:, bass.ds(VCOLS[name][0] + j, 1)]

        def c1(name):
            o, w = CCOLS[name]
            return CON1[:, o:o + w]

        def c2(name):
            o, w = C2COLS[name]
            return CON2[:, o:o + w]

        def unit(ph, i, p):
            L = len(KINDS[ph])
            return UNIT0[ph] + i * L + p, UNIT0[ph] // 4 + i * (L // 4) + p // 4

        def split(ph, i, p):
            k = KINDS[ph]
            n = (k + "s")[:p].count("s")
            return SPLIT0[ph] + i * k.count("s") + n, n % 2

        def halves(ph):
            return ((0, DH), (DH, DT)) if ph == "down" else ((0, 8), (8, 16))

        block = ctx.enter_context(nc.Block())

        @block.sync
        def _(sp):
            def load(ph, i, p, first=False):
                u, u4 = unit(ph, i, p)
                if not first:
                    sp.wait_ge(mm_half, 2 * (u - 3))
                if ph == "down":
                    src = wdown[bass.ds(u - UNIT0[ph], 1)].rearrange("a p t n -> (a p) t n")
                    sp.dma_start(RAW[:, p % 4, 0:DT, :], src).then_inc(raw_full[p % 4], 16)
                else:
                    w = u if UNIT0[ph] < UNIT0["down"] else u - 64
                    src = wts[bass.ds(w, 1)].rearrange("a p t n -> (a p) t n")
                    sp.dma_start(RAW[:, p % 4, :, :], src).then_inc(raw_full[p % 4], 16)

            sp.dma_start(VEC[:], vec).then_inc(in_vec, 16)
            sp.dma_start(CON1[:], con1).then_inc(in_con, 16)
            for p in range(4):
                load("mod1", 0, p, True)
            sp.dma_start(XC[:], xct.rearrange("s (k p) t -> p s k t", p=P)).then_inc(in_x, 16)
            with sp.Fori(1, ITERS["mod1"]) as i:
                for p in range(4):
                    load("mod1", i, p)
            for ph, iters, kinds in PHASES[1:4]:
                with sp.Fori(0, iters) as i:
                    for p in range(len(kinds)):
                        load(ph, i, p)
            sp.wait_ge(ya_ready, 1 + HEADS)
            sp.dma_start(X1[:], xct[0].rearrange("(k p) t -> p k t", p=P)).then_inc(in_x1, 16)
            with sp.Fori(0, ITERS["out"]) as i:
                for p in range(4):
                    load("out", i, p)
            with sp.Fori(0, ITERS["up"]) as i:
                for p in range(4):
                    load("up", i, p)
            sp.wait_ge(x1_out, 16)
            sp.wait_ge(mm_half, 2 * UNIT0["down"])
            sp.dma_start(XF[:], park).then_inc(in_x1b, 16)
            with sp.Fori(0, ITERS["down"]) as i:
                for p in range(8):
                    load("down", i, p)
            sp.wait_ge(mm_half, 2 * UNIT0["attn"])
            sp.dma_start(CON2[:], con2).then_inc(in_con2, 16)
            sp.dma_start(METT[:], metat.rearrange("(k p) t -> p k t", p=P)).then_inc(in_meta, 16)
            with sp.Fori(0, ITERS["attn"]) as i:
                for p in range(8):
                    load("attn", i, p)
            with sp.Fori(0, ITERS["proj"]) as i:
                for p in range(4):
                    load("proj", i, p)

        @block.gpsimd
        def _(pool):
            pool.wait_ge(bank_free, UNIT0["up"])
            pool.dma_start(park, X1[:]).then_inc(x1_out, 16)
            with pool.Fori(0, ITERS["proj"]) as i:
                for p in range(4):
                    pool.wait_ge(bank_free, unit("proj", i, p)[0] + 1)
                    dst = outt[bass.ds(4 * i + p, 1)].rearrange("a p t -> (a p) t")
                    pool.dma_start(dst, OUTS[:, bass.ds(4 * i + p, 1), :].rearrange("p a t -> p (a t)")).then_inc(out_done, 16)
            pool.wait_ge(x1_out, 16)
            pool.wait_ge(out_done, 16 * KD)

        @block.scalar
        def _(act):
            A = nc.scalar
            for one in (kdt_ready, s_ready, lv_exp, h1_aff):
                act.sem_inc(one, 1)
            ch = Chain(act, a_chain)

            def hi(ph, i, p):
                L = len(KINDS[ph])
                if p < L and KINDS[ph][p] == "m":
                    return
                u, u4 = unit(ph, i, p)
                s, slot = split(ph, i, p)
                act.wait_ge(raw_full[p % 4], 16 * (u4 + 1))
                for h, (a, b) in enumerate(halves(ph) if p < L else ((0, 8), (8, 16))):
                    need = 2 if ph == "down" and p == L else h + 1
                    act.wait_ge(mm_half, 2 * (u - 2) + need)
                    A.activation(HI[:, slot, a:b, :], RAW[:, p % 4, a:b, :], ACT.Copy).then_inc(hi_half, 1)

            def done(ph, i, p):
                act.wait_ge(mm_half, 2 * unit(ph, i, p)[0] + 2)

            act.wait_ge(in_vec, 16)
            A.activation(CS[:], VEC[:, VCOLS["c"][0]:VCOLS["c"][0] + 2 * KD].rearrange("p (k s) -> p k s", s=2),
                         ACT.Sigmoid).then_inc(c_sig, 1)
            act.wait_ge(lb_max, 1)
            A.activation(LBV[:, 0:2, :], LBV[:, 0:2, :], ACT.Exp).then_inc(lb_exp, 1)
            act.wait_ge(in_x, 16)
            for g in range(4):
                if g >= 2:
                    act.wait_ge(ss1_mm, g - 1)
                for s in range(2):
                    ins = A.activation(SQ1[:, g % 2, :, s, :], XC[:, s, 4 * g:4 * g + 4, :], ACT.Square)
                ins.then_inc(sq1_done, 1)
            act.wait_ge(ss1_mm, 4)
            act.wait_ge(ones_set, 1)
            ch.link(A.activation(RS1[:].rearrange("p s t -> p (s t)"), AUX[:, 0, :], ACT.Ln, bias=SMALL[:, 0:1]))
            A.activation(RS1[:], RS1[:], ACT.Exp, scale=-0.5).then_inc(rs1_done, 1)
            ch.straight()
            with act.Fori(0, ITERS["mod1"]) as i:
                for p in (0, 1):
                    j = 2 * i + p
                    act.wait_ge(n1_ready, j + 1)
                    for s in range(2):
                        ins = A.activation(HN1[:, s, :], N1[:, s, :], ACT.Identity,
                                           bias=MODV[:, bass.ds(j, 1), s:s + 1].rearrange("p a b -> p (a b)"),
                                           scale=AM1[:, bass.ds(j, 1), s:s + 1].rearrange("p a b -> p (a b)"))
                    ins.then_inc(h1_aff, 1)
            hi("rec", 0, 0)

            with act.Fori(0, ITERS["rec"]) as i:
                for d in (0, 1):
                    hi("rec", i, d + 1)
                    done("rec", i, d)
                    act.wait_ge(bank_free, unit("rec", i, d)[0] - 3)
                    A.activation(SG[:, d].rearrange("p s t -> p (s t)"), ACC[:, d, :], ACT.Sigmoid).then_inc(gate_sig, 1)
                hi("rec", i, 3)
                act.wait_ge(ctx_f, i + 1)
                A.activation(LC[:], LC[:], ACT.Ln).then_inc(ctx_ln, 1)
                act.wait_ge(ctx_scan, i + 1)
                A.activation(EXC[:], EXC[:], ACT.Exp).then_inc(ctx_exp, 1)
                act.wait_ge(kd_tr, 1 + i + 1)
                A.activation(KDT[:].rearrange("p a b -> p (a b)"), AUX[:, 0, :], ACT.Copy).then_inc(kdt_ready, 1)
                hi("rec", i, 4)
                done("rec", i, 3)
                act.wait_ge(bank_free, unit("rec", i, 0)[0])
                A.activation(SGQ[:], ACC[:, 3, 0:T], ACT.Sigmoid).then_inc(gate_sig, 1)
                act.wait_ge(s_mm, 1 + i + 1)
                A.activation(ST[:, :, bass.ds(i, 1), :].rearrange("p s a d -> p s (a d)"),
                             AUX[:, 2, 0:2 * P].rearrange("p (s d) -> p s d", s=2), ACT.Copy).then_inc(s_ready, 1)

            GSIG = 3 * HEADS
            with act.Fori(0, ITERS["mix"]) as i:
                ch.enter(i, CHAIN["a_mix"])

                def level(l):
                    h = 1 << l
                    act.wait_ge(lv_sum, 9 * i + l + 1)
                    act.wait_ge(sc_mm, 1 + 9 * i + (l if l >= 2 else 0))
                    q = QL[:, l % 2].rearrange("p a (n two h) -> p a n two h", two=2, h=h)
                    r = AR[:].rearrange("p a (n two h) -> p a n two h", two=2, h=h)
                    for side, src in ((1, 0), (0, 2)):
                        for a in range(2):
                            ins = A.activation(q[:, a, :, side, :], r[:, src + a, :, side, :], ACT.Exp)
                    ins.then_inc(lv_exp, 1)

                act.wait_ge(f_ready, i + 1)
                A.activation(TT0[:, 0:2, :], TT0[:, 0:2, :], ACT.Ln).then_inc(f_ln, 1)
                level(0)
                done("mix", i, 0)
                act.wait_ge(bank_free, unit("mix", i, 0)[0] - 1)
                A.activation(SGG[:], ACC[:, 0, 0:T], ACT.Sigmoid).then_inc(gate_sig, 1)
                hi("mix", i, 2)
                level(1)
                level(2)
                hi("mix", i, 4)
                level(3)
                level(4)
                hi("mix", i, 6)
                level(5)
                level(6)
                level(7)
                hi("mix", i, 8)
                act.wait_ge(lv_sum, 9 * i + 9)
                for d in range(2):
                    ins = A.activation(QS[:, d, :], AR[:, 2 * d, :], ACT.Exp)
                ins.then_inc(lv_exp, 1)
                act.wait_ge(o_mm, 1 + i + 1)
                for t in range(2):
                    ins = A.activation(OSQ[:, t, :], AUX[:, 3, t * P:(t + 1) * P], ACT.Square,
                                       accum_out=SMALL[:, 4 + t:5 + t])
                ch.link(ins)
                ch.link(A.activation(SMALL[:, 6:8], SMALL[:, 4:6], ACT.Ln, scale=1.0 / P, bias=SMALL[:, 0:1]))
                ch.link(A.activation(SMALL[:, 8:10], SMALL[:, 6:8], ACT.Exp, scale=-0.5))
                A.activation(SMALL[:, 10:12], SMALL[:, 8:10], ACT.Copy).then_inc(o_rstd, 1)
            ch.leave(ITERS["mix"], "a_mix")

            act.wait_ge(ya_ready, 1 + HEADS)
            act.wait_ge(yb_ready, HEADS)
            with act.Fori(0, ITERS["merge"]) as i:
                for jj in range(2):
                    p = 4 * jj
                    hi("merge", i, p + 1)
                    done("merge", i, p)
                    act.wait_ge(bank_free, unit("merge", i, p)[0] - 1)
                    A.activation(GA[:], ACC[:, 0, 0:T], ACT.Sigmoid).then_inc(gate_sig, 1)
                    hi("merge", i, p + 2)
                    done("merge", i, p + 1)
                    A.activation(GB[:], ACC[:, 1, 0:T], ACT.Sigmoid).then_inc(gate_sig, 1)
                    hi("merge", i, p + 4)

            with act.Fori(0, ITERS["out"]) as i:
                for jj in range(2):
                    hi("out", i, 2 * jj + 2)
                    act.wait_ge(bank_free, unit("out", i, 2 * jj)[0] + 1)
                    act.wait_ge(ss2_mm, 1 + 2 * i)
                    A.activation(SQ2[:, jj, :], X1[:, bass.ds(2 * i + jj, 1), :].rearrange("p a t -> p (a t)"),
                                 ACT.Square).then_inc(sq2_done, 1)
            act.wait_ge(ss2_mm, 1 + KD + 1)
            ch.link(A.activation(RS2[:], AUX[:, 0, 0:T], ACT.Ln, bias=SMALL[:, 0:1]))
            A.activation(RS2[:], RS2[:], ACT.Exp, scale=-0.5).then_inc(rs2_done, 1)
            ch.straight()
            for g in range(4):
                act.wait_ge(n2_ready, g + 1)
                for k in range(4):
                    j = 4 * g + k
                    ins = A.activation(N2[:, 4 * (g % 2) + k, :], N2[:, 4 * (g % 2) + k, :], ACT.Identity, bias=MODV[:, 48 + j, 0:1],
                                       scale=AM2[:, j:j + 1])
                ins.then_inc(h2_aff, 1)

            with act.Fori(0, ITERS["up"]) as i:
                for jj in range(2):
                    hi("up", i, 2 * jj + 1)
                    done("up", i, 2 * jj)
                    act.wait_ge(cv_ready, 1 + 2 * i + jj)
                    A.activation(AT[:], ACC[:, 2 * jj, 0:T], ACT.Copy).then_inc(a_copied, 1)
                    hi("up", i, 2 * jj + 2)
                    act.wait_ge(cv_ready, 1 + 2 * i + jj + 1)
                    A.activation(SGU[:], CV[:], ACT.Sigmoid).then_inc(cv_sig, 1)

            with act.Fori(0, ITERS["down"]) as i:
                for jj in range(2):
                    for q in range(4):
                        hi("down", i, 4 * jj + q + 1)
                    act.wait_ge(bank_free, unit("down", i, 4 * jj + 3)[0] + 1)
                    act.wait_ge(ss3_mm, 1 + 2 * i)
                    A.activation(SQ3[:, jj, :], XF[:, bass.ds(2 * i + jj, 1), :].rearrange("p a t -> p (a t)"),
                                 ACT.Square).then_inc(sq3_done, 1)
            act.wait_ge(ss3_mm, 1 + KD + 1)
            ch.link(A.activation(RS2[:], AUX[:, 0, 0:T], ACT.Ln, bias=SMALL[:, 0:1]))
            A.activation(RS2[:], RS2[:], ACT.Exp, scale=-0.5).then_inc(rs3_done, 1)
            ch.straight()
            act.wait_ge(in_meta, 16)
            for k in range(KD):
                act.wait_ge(xf_ready, k + 1)
                if k >= 2:
                    act.wait_ge(ss4_mm, k - 1)
                A.activation(SQ4[:, k % 2, 0:NMETA], METT[:, k, :], ACT.Square)
                A.activation(SQ4[:, k % 2, NMETA:TA], XF[:, k, :], ACT.Square).then_inc(sq4_done, 1)
            act.wait_ge(ss4_mm, KD)
            ch.link(A.activation(RS3[:], AUX[:, 1, 0:TA], ACT.Ln, bias=SMALL[:, 0:1]))
            A.activation(RS3[:], RS3[:], ACT.Exp, scale=-0.5).then_inc(rs4_done, 1)
            ch.straight()
            act.wait_ge(lam_mm, 1)
            A.activation(SMALL[:, 16:18], AUX[:, 2, 0:2], ACT.Exp).then_inc(lam_exp, 1)

            GSIG = GSIG + HEADS + 2 * KD
            with act.Fori(0, ITERS["attn"]) as i:
                ch.enter(i, CHAIN["a_attn"])
                hi("attn", i, 1)
                hi("attn", i, 2)
                act.wait_ge(d_sq, i + 1)
                hi("attn", i, 3)
                act.wait_ge(d_ms, i + 1)
                A.activation(DR[:, 0, 0:T], AUX[:, 0, 0:T], ACT.Ln, bias=SMALL[:, 0:1])
                ch.link(A.activation(DR[:, 1, :], AUX[:, 1, 0:TA], ACT.Ln, bias=SMALL[:, 0:1]))
                A.activation(DR[:, 0, 0:T], DR[:, 0, 0:T], ACT.Exp, scale=-0.5)
                A.activation(DR[:, 1, :], DR[:, 1, :], ACT.Exp, scale=-0.5).then_inc(d_rstd, 1)
                hi("attn", i, 4)
                hi("attn", i, 5)
                act.wait_ge(d_max, i + 1)
                for c in range(2):
                    for t, (a, b) in enumerate(((0, P + NMETA), (P + NMETA, P + NMETA + TA))):
                        ins = A.activation(SS[:, c, a:b], SS[:, c, a:b], ACT.Exp,
                                           bias=ATS[:, 2 * t + c:2 * t + c + 1],
                                           accum_out=ATS[:, 4 + 2 * t + c:5 + 2 * t + c])
                ins.then_inc(d_exp, 1)
                hi("attn", i, 6)
                hi("attn", i, 7)
                act.wait_ge(b_zs, i + 1)
                A.activation(LZ[:], ZS[:], ACT.Abs)
                ch.link(A.activation(LM[0:NMETA, :], ZM[0:NMETA, :], ACT.Abs))
                A.activation(LZ[:], LZ[:], ACT.Exp, scale=-1.0)
                ch.link(A.activation(LM[0:NMETA, :], LM[0:NMETA, :], ACT.Exp, scale=-1.0))
                A.activation(LZ[:], LZ[:], ACT.Ln, bias=SMALL[:, 1:2])
                A.activation(LM[0:NMETA, :], LM[0:NMETA, :], ACT.Ln, bias=SMALL[0:NMETA, 1:2]).then_inc(b_ln, 1)
                act.wait_ge(d_av, 1 + i + 1)
                A.activation(OD[:], AUX[:, 0, 0:T], ACT.Square).then_inc(d_osq, 1)
                act.wait_ge(d_oms, i + 1)
                ch.link(A.activation(RSD[:], AUX[:, 2, 0:T], ACT.Ln, bias=SMALL[:, 2:3]))
                A.activation(RSD[:], RSD[:], ACT.Exp, scale=-0.5).then_inc(d_orstd, 1)
                hi("attn", i, 8)
                act.wait_ge(b_arg, i + 1)
                A.activation(AZ[:], AZ[:], ACT.Exp)
                A.activation(AM[0:NMETA, :], AM[0:NMETA, :], ACT.Exp).then_inc(b_a, 1)
                for g, p in ((0, 6), (1, 7)):
                    done("attn", i, p)
                    A.activation((GSB, GDF)[g][:], ACC[:, p % 4, 0:T], ACT.Sigmoid).then_inc(gate_sig, 1)
            ch.leave(ITERS["attn"], "a_attn")

            with act.Fori(0, ITERS["proj"] - 1) as i:
                for p in range(4):
                    hi("proj", i, p + 1)
            for p in range(3):
                hi("proj", ITERS["proj"] - 1, p + 1)

        @block.tensor
        def _(pe):
            for one in (kd_tr, v_tr, s_mm, sc_mm, o_mm, ss2_mm, ss3_mm, d_sc, dv_tr, d_av, b_z, bv_tr, b_av):
                pe.sem_inc(one, 1)
            def mm(*a, **k):
                return pe.matmul(*a, **k)

            def mod(ph, i, p, cols, first=False):
                u, u4 = unit(ph, i, p)
                pe.wait_ge(raw_full[p % 4], 16 * (u4 + 1))
                if not first:
                    pe.wait_ge(bank_free, u - 3)
                for k in range(KD):
                    ins = mm(ACC[:, p % 4, 0:cols], RAW[:, p % 4, k, :], CS[:, k, 0:cols], start=k == 0, stop=k == KD - 1)
                ins.then_inc(mm_half, 2)

            def prod(ph, i, p, xh, xl, out, groups=None, wait=True, bank_wait=None):
                u, _ = unit(ph, i, p)
                s, slot = split(ph, i, p)
                if bank_wait is None:
                    pe.wait_ge(bank_free, u - 3)
                elif bank_wait is not False:
                    pe.wait_ge(bank_free, bank_wait)
                n = halves(ph)[1][1]
                for h, (a, b) in enumerate(halves(ph)):
                    pe.wait_ge(lo_half, 2 * s + h + 1)
                    for k in range(a, b):
                        first, last = groups(k) if groups else (k == 0, k == n - 1)
                        o = out(k)
                        mm(o, HI[:, slot, k, :], xh(k), start=first, stop=False)
                        mm(o, HI[:, slot, k, :], xl(k), start=False, stop=False)
                        ins = mm(o, LO[:, slot, k, :], xh(k), start=False, stop=last)
                    ins.then_inc(mm_half, 1)

            pe.wait_ge(c_silu, 1)
            for p in range(4):
                mod("mod1", 0, p, 2, True)
            pe.wait_ge(ones_set, 1)
            for g in range(4):
                pe.wait_ge(sq1_done, g + 1)
                for k in range(4):
                    ins = mm(AUX[:, 0, :], ONESR[:], SQ1[:, g % 2, k].rearrange("p s t -> p (s t)"),
                             start=g == 0 and k == 0, stop=g == 3 and k == 3)
                ins.then_inc(ss1_mm, 1)
            with pe.Fori(1, ITERS["mod1"]) as i:
                for p in range(4):
                    mod("mod1", i, p, 2)

            pe.wait_ge(hx_ready, KD)
            with pe.Fori(0, ITERS["rec"]) as i:
                xch, xcl = (lambda k: HX[:, 0:3:2, k, :]), (lambda k: HX[:, 1:4:2, k, :])
                for p in range(3):
                    prod("rec", i, p, xch, xcl, lambda k: ACC[:, p, :].rearrange("p (s t) -> p s t", s=2))
                prod("rec", i, 3, lambda k: HX[:, 0, k, :], lambda k: HX[:, 1, k, :], lambda k: ACC[:, 3, 0:T])
                pe.wait_ge(kd_ready, i + 1)
                pe.wait_ge(kdt_ready, 1 + i)
                for d in range(2):
                    for t in range(2):
                        ins = pe.transpose(AUX[:, 0, (2 * d + t) * P:(2 * d + t + 1) * P], EXC[:, d, t * P:(t + 1) * P], c1("ident"))
                ins.then_inc(kd_tr, 1)
                pe.wait_ge(bank_free, unit("rec", i, 2)[0] + 1)
                pe.wait_ge(vt_ready, 1 + i)
                for s in range(2):
                    for t in range(2):
                        ins = pe.transpose(AUX[:, 1, (2 * s + t) * P:(2 * s + t + 1) * P], VS[:, s, t * P:(t + 1) * P], c1("ident"))
                ins.then_inc(v_tr, 1)
                pe.wait_ge(kdt_ready, 1 + i + 1)
                pe.wait_ge(vt_ready, 1 + i + 1)
                pe.wait_ge(s_ready, 1 + i)
                for d in range(2):
                    for t in range(2):
                        ins = mm(AUX[:, 2, d * P:(d + 1) * P], KDT[:, 2 * d + t, :], VCT[:, t, :], start=t == 0, stop=t == 1)
                ins.then_inc(s_mm, 1)

            pe.wait_ge(s_ready, 1 + HEADS)
            with pe.Fori(0, ITERS["mix"]) as i:
                xh, xl = (lambda k: HX[:, 0, k, :]), (lambda k: HX[:, 1, k, :])

                def tiles(slot, q, k):
                    for t in range(2):
                        ins = mm(AUX[:, t, slot * P:(slot + 1) * P], k[:, t * P:(t + 1) * P], q[:, t * P:(t + 1) * P],
                                 start=True, stop=True)
                    ins.then_inc(sc_mm, 1)

                def level(l):
                    pe.wait_ge(lv_mul, 9 * i + l + 1)
                    tiles((l + 1) % 4, QL[:, l % 2, 0, :], QL[:, l % 2, 1, :])

                prod("mix", i, 0, xh, xl, lambda k: ACC[:, 0, 0:T])
                mod("mix", i, 1, 1)
                pe.wait_ge(ks_ready, i + 1)
                pe.wait_ge(sc_read, 1 + 3 * i)
                tiles(0, QK1[:, 0, :], KS[:])
                prod("mix", i, 2, xh, xl, lambda k: ACC[:, 2, 0:T])
                level(0)
                mod("mix", i, 3, 1)
                level(1)
                level(2)
                prod("mix", i, 4, xh, xl, lambda k: ACC[:, 0, 0:T])
                mod("mix", i, 5, 1)
                pe.wait_ge(sc_read, 1 + 3 * i + 1)
                level(3)
                level(4)
                prod("mix", i, 6, xh, xl, lambda k: ACC[:, 2, 0:T])
                level(5)
                level(6)
                pe.wait_ge(lv_mul, 9 * i + 8)
                pe.wait_ge(ya_ready, 1 + i)
                mm(AUX[:, 2, 0:P], QL[:, 1, 1, 0:P], QL[:, 1, 0, P:T], start=True, stop=True)
                mm(AUX[:, 2, P:T], QL[:, 1, 1, P:T], QL[:, 1, 0, 0:P], start=True, stop=True).then_inc(sc_mm, 1)
                mod("mix", i, 7, 1)
                pe.wait_ge(sc_read, 1 + 3 * i + 3)
                pe.wait_ge(lv_mul, 9 * i + 9)
                for t in range(2):
                    o = AUX[:, 3, t * P:(t + 1) * P]
                    for s in range(2):
                        mm(o, SC[:, s, t * P:(t + 1) * P], VT[:, s, bass.ds(i * P, P)], start=s == 0, stop=False)
                    for d in range(2):
                        ins = mm(o, QS[:, d, t * P:(t + 1) * P], ST[:, d, bass.ds(i, 1), :].rearrange("p a d -> p (a d)"),
                                 start=False, stop=d == 1)
                ins.then_inc(o_mm, 1)
                pe.wait_ge(on_ready, i + 1)
                for t in range(2):
                    ins = pe.transpose(AUX[:, 2, T + t * P:T + (t + 1) * P], ON[:, t, :], c1("ident"))
                ins.then_inc(on_tr, 1)

            pe.wait_ge(ya_ready, 1 + HEADS)
            pe.wait_ge(yb_ready, HEADS)
            with pe.Fori(0, ITERS["merge"]) as i:
                xh, xl = (lambda k: HX[:, 0, k, :]), (lambda k: HX[:, 1, k, :])
                for jj in range(2):
                    p = 4 * jj
                    prod("merge", i, p, xh, xl, lambda k: ACC[:, 0, 0:T])
                    prod("merge", i, p + 1, xh, xl, lambda k: ACC[:, 1, 0:T])
                    prod("merge", i, p + 2, lambda k: YAB[:, 2 * (k // 8), k % 8, :], lambda k: YAB[:, 2 * (k // 8) + 1, k % 8, :],
                         lambda k: ACC[:, 2, (k // 8) * T:(k // 8 + 1) * T], lambda k: (k % 8 == 0, k % 8 == 7))
                    mod("merge", i, p + 3, 1)

            pe.wait_ge(mrg_ready, KD)
            pe.wait_ge(zero_set, 1)
            mm(AUX[:, 0, 0:T], ONESR[:], ZERO[:], start=True, stop=False)
            with pe.Fori(0, ITERS["out"]) as i:
                for jj in range(2):
                    prod("out", i, 2 * jj, lambda k: MRG[:, 0, k, :], lambda k: MRG[:, 1, k, :], lambda k: ACC[:, 2 * jj, 0:T])
                    mod("out", i, 2 * jj + 1, 1)
                for jj in range(2):
                    pe.wait_ge(sq2_done, 2 * i + jj + 1)
                    mm(AUX[:, 0, 0:T], ONESR[:], SQ2[:, jj, :], start=False, stop=False).then_inc(ss2_mm, 1)
            mm(AUX[:, 0, 0:T], ONESR[:], ZERO[:], start=False, stop=True).then_inc(ss2_mm, 1)

            pe.wait_ge(hx2_ready, 4)
            with pe.Fori(0, ITERS["up"]) as i:
                for p in range(4):
                    prod("up", i, p, lambda k: HX[:, 0, k, :], lambda k: HX[:, 1, k, :], lambda k: ACC[:, p, 0:T])

            pe.wait_ge(s_hidden, FF)
            pe.wait_ge(bank_free, UNIT0["down"])
            mm(AUX[:, 0, 0:T], ONESR[:], ZERO[:], start=True, stop=False)
            with pe.Fori(0, ITERS["down"]) as i:
                for jj in range(2):
                    for q in range(4):
                        p = 4 * jj + q
                        u = unit("down", i, p)[0]
                        prod("down", i, p, lambda k: SH[:, DT * q + k, :], lambda k: SL[:, DT * q + k, :],
                             lambda k: ACC[:, jj, 0:T], lambda k: (q == 0 and k == 0, q == 3 and k == DT - 1),
                             bank_wait=u - 4 if q == 0 else False)
                for jj in range(2):
                    pe.wait_ge(sq3_done, 2 * i + jj + 1)
                    mm(AUX[:, 0, 0:T], ONESR[:], SQ3[:, jj, :], start=False, stop=False).then_inc(ss3_mm, 1)
            mm(AUX[:, 0, 0:T], ONESR[:], ZERO[:], start=False, stop=True).then_inc(ss3_mm, 1)

            for k in range(KD):
                pe.wait_ge(sq4_done, k + 1)
                mm(AUX[:, 1, 0:TA], ONESR[:], SQ4[:, k % 2, :], start=k == 0, stop=k == KD - 1).then_inc(ss4_mm, 1)
            pe.wait_ge(lam_prod, 1)
            pe.wait_ge(at_const, 1)
            mm(AUX[:, 2, 0:2], ONEP[:], SMALL[:, 14:16], start=True, stop=True).then_inc(lam_mm, 1)
            pe.wait_ge(in_con2, 16)
            pe.wait_ge(u2_ready, 4)
            pe.wait_ge(lam_exp, 1)
            with pe.Fori(0, ITERS["attn"]) as i:
                def proj(p, meta):
                    a = 0 if meta else NMETA
                    prod("attn", i, p, lambda k: U2[:, 0, k, a:TA], lambda k: U2[:, 1, k, a:TA],
                         lambda k: ACC[:, p % 4, 0:TA - a])

                def tokens_major(src, bank):
                    for n, (a, w) in enumerate(((NMETA, P), (NMETA + P, P), (0, NMETA))):
                        ins = pe.transpose(AUX[0:w, bank, n * P:(n + 1) * P], src[:, a:a + w], c1("ident"))
                    return ins

                proj(0, False)
                proj(1, True)
                proj(2, True)
                pe.wait_ge(d_sq, i + 1)
                pe.wait_ge(mix_ready, 1 + 2 * i)
                mm(AUX[:, 0, 0:T], c2("blk64"), DR[:, 0, 0:T], start=True, stop=True)
                mm(AUX[:, 1, 0:TA], c2("blk64"), DR[:, 1, :], start=True, stop=True).then_inc(d_ms, 1)
                proj(3, False)
                pe.wait_ge(bank_free, unit("attn", i, 2)[0] + 1)
                tokens_major(DV, 2).then_inc(dv_tr, 1)
                pe.wait_ge(d_norm, i + 1)
                mm(AUX[:, 0, 0:T], c2("rot"), DN[:, 0, 0:T], start=True, stop=True)
                mm(AUX[:, 1, 0:TA], c2("rot"), DN[:, 1, :], start=True, stop=True).then_inc(d_rot, 1)
                proj(4, True)
                pe.wait_ge(d_rope, i + 1)
                for c in range(2):
                    r = slice(64 * c, 64 * c + 64)
                    mm(AUX[:, c, 0:P + NMETA], DQK[r, 0, 0:P], DQK[r, 1, 0:P + NMETA], start=True, stop=True)
                    ins = mm(AUX[:, c, P + NMETA:P + NMETA + TA], DQK[r, 0, P:T], DQK[r, 1, :], start=True, stop=True)
                ins.then_inc(d_sc, 1)
                proj(5, True)
                pe.wait_ge(bank_free, unit("attn", i, 5)[0] + 1)
                pe.wait_ge(dvt_ready, i + 1)
                tokens_major(SV, 2).then_inc(bv_tr, 1)
                pe.wait_ge(d_max, i + 1)
                mm(AUX[:, 1, 0:T], SKF[:, NMETA:NMETA + P], SQF[:], start=True, stop=True)
                mm(AUX[:, 1, T:T + P], SKF[:, NMETA + P:TA], SQF[:, P:T], start=True, stop=True)
                pe.wait_ge(svt_ready, i + 1)
                mm(AUX[0:NMETA, 2, 0:T], SKF[:, 0:NMETA], SQF[:], start=True, stop=True).then_inc(b_z, 1)
                pe.wait_ge(d_w, i + 1)
                q1 = P + NMETA
                for n, a in enumerate((NMETA, q1 + NMETA, q1 + NMETA + P)):
                    pe.transpose(AUX[:, 3, n * P:(n + 1) * P], SS[:, 0, a:a + P], c1("ident"))
                for n, a in enumerate((0, q1)):
                    ins = pe.transpose(AUX[0:NMETA, 0, n * P:(n + 1) * P], SS[:, 0, a:a + NMETA], c1("ident"))
                ins.then_inc(d_wtr, 1)
                proj(6, False)
                pe.wait_ge(d_wt, i + 1)
                mm(AUX[:, 0, 0:T], DVT[0:NMETA, 2, :], WTM[0:NMETA, :], start=True, stop=False)
                mm(AUX[:, 0, 0:T], DVT[:, 0, :], WTS[:, 0:T], start=False, stop=False)
                mm(AUX[:, 0, P:T], DVT[:, 1, :], WTS[:, T:T + P], start=False, stop=True).then_inc(d_av, 1)
                pe.wait_ge(b_sp, i + 1)
                mm(AUX[:, 1, 0:T], c2("tri"), LZ[:, 0:T], start=True, stop=False)
                mm(AUX[:, 1, P:T], ONEP[:], LZ[:, T:T + P], start=False, stop=True)
                mm(AUX[:, 1, T:T + P], c2("tri"), LZ[:, T:T + P], start=True, stop=True)
                mm(AUX[0:NMETA, 3, 0:T], c2("tri")[0:NMETA, 0:NMETA], LM[0:NMETA, :], start=True, stop=False)
                mm(AUX[0:NMETA, 3, 0:T], ONEP[:, 0:NMETA], LZ[:, 0:T], start=False, stop=False)
                mm(AUX[0:NMETA, 3, P:T], ONEP[:, 0:NMETA], LZ[:, T:T + P], start=False, stop=True).then_inc(b_tail, 1)
                pe.wait_ge(d_osq, i + 1)
                mm(AUX[:, 2, 0:T], ON128[:], OD[:], start=True, stop=True).then_inc(d_oms, 1)
                proj(7, False)
                pe.wait_ge(b_a, i + 1)
                mm(AUX[:, 3, 0:T], SVT[0:NMETA, 2, :], AM[0:NMETA, :], start=True, stop=False)
                mm(AUX[:, 3, 0:T], SVT[:, 0, :], AZ[:, 0:T], start=False, stop=False)
                mm(AUX[:, 3, P:T], SVT[:, 1, :], AZ[:, T:T + P], start=False, stop=True).then_inc(b_av, 1)

            pe.wait_ge(mix_ready, 1 + 2 * HEADS)
            with pe.Fori(0, ITERS["proj"]) as i:
                for p in range(4):
                    prod("proj", i, p, lambda k: MIX[:, 0, k, :], lambda k: MIX[:, 1, k, :], lambda k: ACC[:, p, 0:T])

        @block.vector
        def _(dve):
            V = nc.vector
            for one in (vt_ready, sc_read, ya_ready, cv_ready, mix_ready):
                dve.sem_inc(one, 1)
            ch = Chain(dve, v_chain)
            link, mark = ch.link, ch.mark

            def lo(ph, i, p):
                L = len(KINDS[ph])
                if p < L and KINDS[ph][p] == "m":
                    return
                s, slot = split(ph, i, p)
                for h, (a, b) in enumerate(halves(ph) if p < L else ((0, 8), (8, 16))):
                    dve.wait_ge(hi_half, 2 * s + h + 1)
                    V.tensor_tensor(LO[:, slot, a:b, :], RAW[:, p % 4, a:b, :], HI[:, slot, a:b, :].bitcast(F32),
                                    ALU.subtract).then_inc(lo_half, 1)

            def done(ph, i, p):
                dve.wait_ge(mm_half, 2 * unit(ph, i, p)[0] + 2)

            def modv(ph, i, p, idx, cols, chain=False):
                done(ph, i, p)
                for s in range(cols):
                    ins = V.tensor_scalar(MODV[:, bass.ds(idx, 1), s:s + 1].rearrange("p a b -> p (a b)"),
                                          ACC[:, p % 4, s:s + 1], vcd("bmod", idx), None, ALU.add)
                ins.then_inc(bank_free, 1)

            def split_small(dst_hi, dst_lo, src, ready=None):
                link(V.tensor_copy(dst_hi, src))
                ins = V.tensor_tensor(dst_lo, src, dst_hi.bitcast(F32), ALU.subtract)
                return ins

            V.memset(SMALL[:], 0.0)
            V.memset(ONESR[:], 1.0 / D)
            link(V.memset(ONE[:], 1.0))
            V.memset(SMALL[:, 0:1], EPS)
            V.memset(SMALL[:, 1:2], 1.0)
            V.memset(SMALL[:, 2:3], SUBLN_EPS).then_inc(ones_set, 1)
            dve.wait_ge(in_vec, 16)
            r0, r1 = vc("lb", 0, 16), vc("lb", 16, 16)
            link(V.tensor_tensor(LBV[:, 2, :], r0, r1, ALU.max))
            V.tensor_tensor(LBV[:, 0, :], r0, LBV[:, 2, :], ALU.subtract)
            V.tensor_tensor(LBV[:, 1, :], r1, LBV[:, 2, :], ALU.subtract).then_inc(lb_max, 1)
            dve.wait_ge(c_sig, 1)
            V.tensor_tensor(CS[:], CS[:], vc("c", 0, 2 * KD).rearrange("p (k s) -> p k s", s=2), ALU.mult).then_inc(c_silu, 1)
            dve.wait_ge(lb_exp, 1)
            link(V.tensor_tensor(LBV[:, 2, :], LBV[:, 0, :], LBV[:, 1, :], ALU.add))
            link(V.reciprocal(LBV[:, 2, :], LBV[:, 2, :]))
            link(V.tensor_tensor(LBV[:, 0, :], LBV[:, 0, :], LBV[:, 2, :], ALU.mult))
            link(V.tensor_scalar(LBV[:, 1, :], LBV[:, 0, :], -1.0, 1.0, ALU.mult, ALU.add))
            ch.straight()
            dve.wait_ge(rs1_done, 1)
            with dve.Fori(0, ITERS["mod1"]) as i:
                ch.enter(i, CHAIN["v_mod1"])
                for b in range(2):
                    j = 2 * i + b
                    modv("mod1", i, 2 * b, j, 2)
                    done("mod1", i, 2 * b + 1)
                    for s in range(2):
                        ins = V.tensor_scalar(SMALL[:, 12 + s:13 + s], ACC[:, 2 * b + 1, s:s + 1],
                                              vcd("bmod", KD + j), 1.0, ALU.add, ALU.add)
                        if s == 0:
                            mark(ins)
                    ins.then_inc(bank_free, 1)
                    ch.wait()
                    dve.wait_ge(bank_free, unit("mod1", i, 2 * b + 1)[0] + 1)
                    am = AM1[:, bass.ds(j, 1), :].rearrange("p a s -> p (a s)")
                    link(V.tensor_scalar(am, SMALL[:, 12:14], vcd("norm1", j), None, ALU.mult))
                    dve.wait_ge(h1_aff, 1 + j)
                    V.tensor_tensor(N1[:], XC[:, :, bass.ds(j, 1), :].rearrange("p s a t -> p s (a t)"), RS1[:],
                                    ALU.mult).then_inc(n1_ready, 1)
                    dve.wait_ge(h1_aff, 1 + j + 1)
                    hh = HX[:, 0:3:2, bass.ds(j, 1), :].rearrange("p s a t -> p s (a t)")
                    hl = HX[:, 1:4:2, bass.ds(j, 1), :].rearrange("p s a t -> p s (a t)")
                    link(V.tensor_copy(hh, HN1[:]))
                    V.tensor_tensor(hl, HN1[:], hh.bitcast(F32), ALU.subtract).then_inc(hx_ready, 1)
            ch.leave(ITERS["mod1"], "v_mod1")
            lo("rec", 0, 0)

            with dve.Fori(0, ITERS["rec"]) as i:
                ch.enter(i, CHAIN["v_rec"])

                def head(t, d):
                    return t[:, d, bass.ds(i, 1), :].rearrange("p a t -> p (a t)")

                def gate(d):
                    dve.wait_ge(gate_sig, 3 * i + d + 1)
                    l0 = LBV[:, 0, bass.ds(HEADS * d + i, 1)]
                    l1 = LBV[:, 1, bass.ds(HEADS * d + i, 1)]
                    mark(V.tensor_scalar(head(FG, d), SG[:, d, 0, :], l1, l0, ALU.mult, ALU.add))
                    V.tensor_scalar(FC[:, d, :], SG[:, d, 1, :], l1, l0, ALU.mult, ALU.add).then_inc(bank_free, 1)

                lo("rec", i, 1)
                gate(0)
                lo("rec", i, 2)
                gate(1)
                ch.wait()
                dve.wait_ge(bank_free, unit("rec", i, 1)[0] + 1)
                link(V.tensor_scalar(LC[:], FC[:], TINY, None, ALU.max))
                V.tensor_scalar(FC[:], FC[:], -1.0, 1.0, ALU.mult, ALU.add).then_inc(ctx_f, 1)
                lo("rec", i, 3)
                dve.wait_ge(ctx_ln, i + 1)
                dve.wait_ge(kd_tr, 1 + i)
                V.memset(EXC[:, 0, T - 1:T], 0.0)
                mark(V.memset(EXC[:, 1, 0:1], 0.0))
                mark(V.tensor_tensor_scan(EXC[:, 0, 0:T - 1][:, ::-1], ONE[:, 0:T - 1], LC[:, 0, 1:T][:, ::-1], 0.0,
                                          ALU.mult, ALU.add))
                V.tensor_tensor_scan(EXC[:, 1, 1:T], ONE[:, 0:T - 1], LC[:, 1, 0:T - 1], 0.0,
                                     ALU.mult, ALU.add).then_inc(ctx_scan, 1)
                done("rec", i, 2)
                dve.wait_ge(v_tr, 1 + i)
                V.tensor_copy(VS[:].rearrange("p s t -> p (s t)"), ACC[:, 2, :]).then_inc(bank_free, 1)
                dve.wait_ge(ctx_exp, i + 1)
                dve.wait_ge(ctx_f, i + 1)
                V.tensor_tensor(EXC[:], EXC[:], FC[:], ALU.mult).then_inc(kd_ready, 1)
                lo("rec", i, 4)
                dve.wait_ge(v_tr, 1 + i + 1)
                dve.wait_ge(s_mm, 1 + i)
                mark(V.tensor_copy(VCT[:].rearrange("p t d -> p (t d)"), AUX[:, 1, T:2 * T]))
                V.tensor_copy(VT[:, :, bass.ds(i * P, P)], AUX[:, 1, 0:T].rearrange("p (t d) -> p t d", t=2)).then_inc(vt_ready, 1)
                dve.wait_ge(gate_sig, 3 * i + 3)
                V.tensor_tensor(QF[:, bass.ds(i, 1), :].rearrange("p a t -> p (a t)"), ACC[:, 3, 0:T], SGQ[:],
                                ALU.mult).then_inc(bank_free, 1)
            ch.leave(ITERS["rec"], "v_rec")

            GSIG = 3 * HEADS
            link(V.memset(UP[:], 0.0))
            ch.straight()
            dve.wait_ge(vt_ready, 1 + HEADS)
            dve.wait_ge(s_mm, 1 + HEADS)
            dve.wait_ge(bank_free, UNIT0["mix"])
            with dve.Fori(0, ITERS["mix"]) as i:
                ch.enter(i, CHAIN["v_mix"])

                def totals(l, n):
                    return (TT0, TT1)[l % 2][:, :, 0:n]

                def level(l):
                    h = 1 << l
                    nb = T // (2 * h)
                    dve.wait_ge(lv_exp, 1 + 9 * i + l + 1)
                    q = QL[:, l % 2].rearrange("p a (n two h) -> p a n two h", two=2, h=h)
                    for side, src in ((1, QK1), (0, QK0)):
                        o = src[:].rearrange("p a (n two h) -> p a n two h", two=2, h=h)
                        ins = V.tensor_tensor(q[:, :, :, side, :], q[:, :, :, side, :], o[:, :, :, side, :], ALU.mult)
                    ins.then_inc(lv_mul, 1)
                    r = AR[:].rearrange("p a (n two h) -> p a n two h", two=2, h=h)
                    tt = totals(l, 2 * nb).rearrange("p a (n two) -> p a n two", two=2)
                    right, left = r[:, 0:2, :, 1, :], r[:, 2:4, :, 0, :]
                    if l < LEVELS - 1:
                        mark(V.tensor_tensor(totals(l + 1, nb), tt[:, :, :, 0], tt[:, :, :, 1], ALU.add))
                    mark(V.tensor_tensor(right, right, tt[:, 0:2, :, 0].unsqueeze(3).broadcast_to([P, 2, nb, h]), ALU.add))
                    V.tensor_tensor(left, left, tt[:, 1:3, :, 1].unsqueeze(3).broadcast_to([P, 2, nb, h]),
                                    ALU.add).then_inc(lv_sum, 1)
                    ch.wait()
                    dve.wait_ge(lv_sum, 9 * i + l + 2)

                def mask(g, out):
                    dve.wait_ge(sc_mm, 1 + 9 * i + 4 * g + 4)
                    m = c1("masks")[:, 4 * g * P:4 * (g + 1) * P].unsqueeze(1).broadcast_to([P, 2, 4 * P])
                    V.tensor_tensor(SCT[:].rearrange("p t s n -> p t (s n)"), AUX[:, 0:2, :], m, ALU.mult).then_inc(sc_read, 1)
                    dve.wait_ge(sc_read, 1 + 3 * i + g + 1)
                    for t in range(2):
                        ins = V.tensor_reduce(out(t), SCT[:, t].rearrange("p s n -> p n s"), AX.X, ALU.add)
                        mark(ins)
                    ch.wait()

                x = lambda t, d: t[:, d, bass.ds(i, 1), :].rearrange("p a t -> p (a t)")
                qf = QF[:, bass.ds(i, 1), :].rearrange("p a t -> p (a t)")
                V.tensor_scalar(TT0[:, 0:2, :], FG[:, :, bass.ds(i, 1), :].rearrange("p d a t -> p d (a t)"), TINY, None,
                                ALU.max).then_inc(f_ready, 1)
                dve.wait_ge(sc_mm, 1 + 9 * i)
                mark(V.tensor_scalar(QK0[:, 1, :], x(FG, 0), -1.0, 1.0, ALU.mult, ALU.add))
                mark(V.tensor_scalar(QK1[:, 1, :], x(FG, 1), -1.0, 1.0, ALU.mult, ALU.add))
                mark(V.tensor_copy(QK0[:, 0, :], qf))
                mark(V.tensor_copy(QK1[:, 0, :], qf))
                ch.wait()
                V.tensor_tensor(KS[:], QK0[:, 1, :], QK1[:, 1, :], ALU.add).then_inc(ks_ready, 1)
                dve.wait_ge(lv_exp, 1 + 9 * i)
                mark(V.memset(AR[:, 1, :], 0.0))
                mark(V.memset(AR[:, 3, :], 0.0))
                dve.wait_ge(f_ln, i + 1)
                mark(V.tensor_copy(AR[:, 0, :], TT0[:, 0, :]))
                mark(V.tensor_copy(AR[:, 2, :], TT0[:, 1, :]))
                ch.wait()
                V.tensor_copy(TT0[:, 2, :], TT0[:, 0, :]).then_inc(lv_sum, 1)
                dve.wait_ge(lv_sum, 9 * i + 1)
                level(0)
                dve.wait_ge(gate_sig, GSIG + i + 1)
                V.tensor_tensor(GS[:], ACC[:, 0, 0:T], SGG[:], ALU.mult).then_inc(bank_free, 1)
                lo("mix", i, 2)
                level(1)
                modv("mix", i, 1, 48 + 4 * i, 1)
                level(2)
                done("mix", i, 2)
                V.tensor_copy(SCB[:], ACC[:, 2, 0:T]).then_inc(bank_free, 1)
                lo("mix", i, 4)
                level(3)
                modv("mix", i, 3, 49 + 4 * i, 1)
                dve.wait_ge(o_mm, 1 + i)
                mask(0, lambda t: SC[:, t, t * P:(t + 1) * P])
                level(4)
                done("mix", i, 4)
                V.tensor_tensor(UP[:, 1:T + 1], ACC[:, 0, 0:T], SCB[:], ALU.mult).then_inc(bank_free, 1)
                lo("mix", i, 6)
                dve.wait_ge(bank_free, unit("mix", i, 4)[0] + 1)
                w = lambda n: vcd("sconv", HEADS * n + i)
                link(V.tensor_scalar(SGG[:], UP[:, 1:T + 1], w(1), None, ALU.mult))
                link(V.scalar_tensor_tensor(SGG[:], UP[:, 0:T], w(0), SGG[:], ALU.mult, ALU.add))
                link(V.scalar_tensor_tensor(SGG[:], UP[:, 2:T + 2], w(2), SGG[:], ALU.mult, ALU.add))
                modv("mix", i, 5, 50 + 4 * i, 1)
                level(5)
                level(6)
                done("mix", i, 6)
                V.tensor_tensor(SCB[:], ACC[:, 2, 0:T], SGG[:], ALU.mult).then_inc(bank_free, 1)
                lo("mix", i, 8)
                dve.wait_ge(bank_free, unit("mix", i, 6)[0] + 1)
                split_small(x(YAB, 2), x(YAB, 3), SCB[:]).then_inc(yb_ready, 1)
                level(7)
                modv("mix", i, 7, 51 + 4 * i, 1)
                dve.wait_ge(lv_exp, 1 + 9 * i + 9)
                V.tensor_tensor(QS[:], QS[:], qf.unsqueeze(1).broadcast_to([P, 2, T]), ALU.mult).then_inc(lv_mul, 1)
                mask(1, lambda t: KS[:, t * P:(t + 1) * P])
                for t in range(2):
                    d = SC[:, t, t * P:(t + 1) * P]
                    mark(V.tensor_tensor(d, d, KS[:, t * P:(t + 1) * P], ALU.add))
                dve.wait_ge(sc_mm, 1 + 9 * i + 9)
                mark(V.tensor_copy(SC[:, 0, P:T], AUX[:, 2, 0:P]))
                V.tensor_copy(SC[:, 1, 0:P], AUX[:, 2, P:T]).then_inc(sc_read, 1)
                dve.wait_ge(o_rstd, i + 1)
                mark(V.tensor_scalar(ON[:, 0, :], AUX[:, 3, 0:P], SMALL[:, 10:11], None, ALU.mult))
                V.tensor_scalar(ON[:, 1, :], AUX[:, 3, P:T], SMALL[:, 11:12], None, ALU.mult).then_inc(on_ready, 1)
                dve.wait_ge(on_tr, i + 1)
                link(V.scalar_tensor_tensor(YT[:], AUX[:, 2, T:2 * T], vc("anorm"), GS[:], ALU.mult, ALU.mult))
                split_small(x(YAB, 0), x(YAB, 1), YT[:]).then_inc(ya_ready, 1)
            ch.leave(ITERS["mix"], "v_mix")
            GSIG += HEADS

            dve.wait_ge(ya_ready, 1 + HEADS)
            with dve.Fori(0, ITERS["merge"]) as i:
                ch.enter(i, CHAIN["v_merge"])
                for jj in range(2):
                    p, j = 4 * jj, 2 * i + jj
                    lo("merge", i, p + 1)
                    lo("merge", i, p + 2)
                    done("merge", i, p + 2)
                    dve.wait_ge(gate_sig, GSIG + 2 * j + 2)
                    V.tensor_tensor(M1[:], ACC[:, 2, 0:T], GA[:], ALU.mult).then_inc(bank_free, 1)
                    V.tensor_tensor(M2[:], ACC[:, 2, T:2 * T], GB[:], ALU.mult).then_inc(bank_free, 1)
                    lo("merge", i, p + 4)
                    dve.wait_ge(bank_free, unit("merge", i, p + 2)[0])
                    V.tensor_tensor(M1[:], M1[:], M2[:], ALU.add).then_inc(bank_free, 1)
                    dve.wait_ge(bank_free, unit("merge", i, p + 2)[0] + 1)
                    o = lambda s: MRG[:, s, bass.ds(j, 1), :].rearrange("p a t -> p (a t)")
                    link(V.tensor_copy(o(0), M1[:]))
                    V.tensor_tensor(o(1), M1[:], o(0).bitcast(F32), ALU.subtract).then_inc(mrg_ready, 1)
                    modv("merge", i, p + 3, 32 + j, 1)
            ch.leave(ITERS["merge"], "v_merge")
            GSIG += 2 * KD

            dve.wait_ge(mrg_ready, KD)
            V.memset(ZERO[:], 0.0).then_inc(zero_set, 1)
            dve.wait_ge(in_x1, 16)
            with dve.Fori(0, ITERS["out"]) as i:
                for jj in range(2):
                    j = 2 * i + jj
                    lo("out", i, 2 * jj + 2)
                    done("out", i, 2 * jj)
                    x1 = X1[:, bass.ds(j, 1), :].rearrange("p a t -> p (a t)")
                    g1 = MODV[:, bass.ds(32 + j, 1), 0:1].rearrange("p a b -> p (a b)")
                    V.scalar_tensor_tensor(x1, ACC[:, 2 * jj, 0:T], g1, x1, ALU.mult, ALU.add).then_inc(bank_free, 1)
                    modv("out", i, 2 * jj + 1, 80 + j, 1)
            dve.wait_ge(bank_free, UNIT0["up"])
            link(V.scalar_tensor_tensor(AM2[:], MODV[:, 64:80, 0], 1.0, vc("norm2", 0, KD), ALU.add, ALU.mult))
            dve.wait_ge(rs2_done, 1)
            for g in range(5):
                if g < 4:
                    V.tensor_tensor(N2[:, 4 * (g % 2):4 * (g % 2) + 4, :], X1[:, 4 * g:4 * g + 4, :],
                                    RS2[:].unsqueeze(1).broadcast_to([P, 4, T]), ALU.mult).then_inc(n2_ready, 1)
                if g > 0:
                    n = N2[:, 4 * ((g - 1) % 2):4 * ((g - 1) % 2) + 4, :]
                    dve.wait_ge(h2_aff, g)
                    split_small(HX[:, 0, 4 * g - 4:4 * g, :], HX[:, 1, 4 * g - 4:4 * g, :], n).then_inc(hx2_ready, 1)
                    dve.wait_ge(hx2_ready, g)
            ch.straight()

            dve.wait_ge(x1_out, 16)
            with dve.Fori(0, ITERS["up"]) as i:
                ch.enter(i, CHAIN["v_up"])
                for jj in range(2):
                    j = 2 * i + jj
                    w = lambda r, c: vcd("dw", FF * (3 * r + c) + j)
                    at4, cv4 = (t[:].rearrange("p (r c) -> p r c", c=GRID) for t in (AT, CV))
                    lo("up", i, 2 * jj + 1)
                    dve.wait_ge(a_copied, j + 1)
                    V.tensor_scalar(CV[:], AT[:], w(1, 1), vcd("db", j), ALU.mult, ALU.add).then_inc(bank_free, 1)
                    lo("up", i, 2 * jj + 2)
                    dve.wait_ge(bank_free, unit("up", i, 2 * jj)[0] + 1)
                    for r in range(3):
                        for c in range(3):
                            if (r, c) == (1, 1):
                                continue
                            y0, y1 = max(0, 1 - r), min(4, 5 - r)
                            x0, x1 = max(0, 1 - c), min(GRID, GRID + 1 - c)
                            o = cv4[:, y0:y1, x0:x1]
                            ins = V.scalar_tensor_tensor(o, at4[:, y0 + r - 1:y1 + r - 1, x0 + c - 1:x1 + c - 1],
                                                         w(r, c), o, ALU.mult, ALU.add)
                            if (r, c) == (2, 2):
                                ins.then_inc(cv_ready, 1)
                            else:
                                link(ins)
                    dve.wait_ge(cv_ready, 1 + j + 1)
                    dve.wait_ge(cv_sig, j + 1)
                    link(V.tensor_tensor(S1[:], CV[:], SGU[:], ALU.mult))
                    done("up", i, 2 * jj + 1)
                    V.tensor_tensor(S1[:], ACC[:, 2 * jj + 1, 0:T], S1[:], ALU.mult).then_inc(bank_free, 1)
                    dve.wait_ge(bank_free, unit("up", i, 2 * jj + 1)[0] + 1)
                    o = lambda t: t[:, bass.ds(j, 1), :].rearrange("p a t -> p (a t)")
                    split_small(o(SH), o(SL), S1[:]).then_inc(s_hidden, 1)
            ch.leave(ITERS["up"], "v_up")

            dve.wait_ge(in_x1b, 16)
            with dve.Fori(0, ITERS["down"]) as i:
                for jj in range(2):
                    j = 2 * i + jj
                    for q in range(4):
                        lo("down", i, 4 * jj + q + 1)
                    done("down", i, 4 * jj + 3)
                    xf = XF[:, bass.ds(j, 1), :].rearrange("p a t -> p (a t)")
                    g2 = MODV[:, bass.ds(80 + j, 1), 0:1].rearrange("p a b -> p (a b)")
                    V.scalar_tensor_tensor(xf, ACC[:, jj, 0:T], g2, xf, ALU.mult, ALU.add).then_inc(bank_free, 4)
            dve.wait_ge(bank_free, UNIT0["attn"])
            V.memset(ONEP[:], 1.0)
            V.memset(ON128[:], 1.0 / P).then_inc(at_const, 1)
            o = VCOLS["lam"][0]
            V.tensor_tensor(SMALL[:, 14:16], VEC[:, o:o + 2], VEC[:, o + 2:o + 4], ALU.mult).then_inc(lam_prod, 1)
            mark(V.tensor_scalar(SMALL[:, 20:21], vc("subln"), 1.0 - LAM_INIT, None, ALU.mult))
            dve.wait_ge(rs3_done, 1)
            for k in range(KD):
                V.scalar_tensor_tensor(XF[:, k, :], XF[:, k, :], vc("final", k), RS2[:], ALU.mult, ALU.mult).then_inc(xf_ready, 1)
            dve.wait_ge(xf_ready, KD)
            dve.wait_ge(in_meta, 16)
            dve.wait_ge(rs4_done, 1)
            for g in range(4):
                for k in range(4 * g, 4 * g + 4):
                    mark(V.scalar_tensor_tensor(N3[:, k % 4, 0:NMETA], METT[:, k, :], vc("norm_2", k), RS3[:, 0:NMETA],
                                                ALU.mult, ALU.mult))
                    mark(V.scalar_tensor_tensor(N3[:, k % 4, NMETA:TA], XF[:, k, :], vc("norm_2", k), RS3[:, NMETA:TA],
                                                ALU.mult, ALU.mult))
                ch.wait()
                split_small(U2[:, 0, 4 * g:4 * g + 4, :], U2[:, 1, 4 * g:4 * g + 4, :], N3[:]).then_inc(u2_ready, 1)
                dve.wait_ge(u2_ready, g + 1)
            dve.wait_ge(lam_exp, 1)
            link(V.tensor_tensor(SMALL[:, 18:19], SMALL[:, 16:17], SMALL[:, 17:18], ALU.subtract))
            link(V.tensor_scalar(SMALL[:, 19:20], SMALL[:, 18:19], LAM_INIT, None, ALU.add))
            ch.straight()

            dve.wait_ge(in_con2, 16)
            sc = float(P) ** -0.5
            q1 = P + NMETA
            with dve.Fori(0, ITERS["attn"]) as i:
                ch.enter(i, CHAIN["v_attn"])

                def take(p, dst, n):
                    done("attn", i, p)
                    V.tensor_copy(dst, ACC[:, p % 4, 0:n]).then_inc(bank_free, 1)

                def mixed(g):
                    o = lambda s: MIX[:, s, bass.ds(HEADS * g + i, 1), :].rearrange("p a t -> p (a t)")
                    split_small(o(0), o(1), MT[:]).then_inc(mix_ready, 1)

                lo("attn", i, 1)
                dve.wait_ge(d_sc, 1 + i)
                take(0, DQK[:, 0, 0:T], T)
                lo("attn", i, 2)
                take(1, DQK[:, 1, :], TA)
                dve.wait_ge(bank_free, unit("attn", i, 1)[0] + 1)
                mark(V.tensor_tensor(DR[:, 0, 0:T], DQK[:, 0, 0:T], DQK[:, 0, 0:T], ALU.mult))
                V.tensor_tensor(DR[:, 1, :], DQK[:, 1, :], DQK[:, 1, :], ALU.mult).then_inc(d_sq, 1)
                lo("attn", i, 3)
                dve.wait_ge(dv_tr, 1 + i)
                take(2, DV[:], TA)
                dve.wait_ge(d_rstd, i + 1)
                mark(V.scalar_tensor_tensor(DN[:, 0, 0:T], DQK[:, 0, 0:T], vc("qn"), DR[:, 0, 0:T], ALU.mult, ALU.mult))
                V.scalar_tensor_tensor(DN[:, 1, :], DQK[:, 1, :], vc("kn"), DR[:, 1, :], ALU.mult, ALU.mult).then_inc(d_norm, 1)
                lo("attn", i, 4)
                dve.wait_ge(dv_tr, 1 + i + 1)
                dve.wait_ge(d_av, 1 + i)
                mark(V.tensor_copy(DVT[:, 0:2, :].rearrange("p a d -> p (a d)"), AUX[:, 2, 0:T]))
                V.tensor_copy(DVT[0:NMETA, 2, :], AUX[0:NMETA, 2, T:T + P]).then_inc(dvt_ready, 1)
                ch.wait()
                dve.wait_ge(d_norm, i + 1)
                mark(V.tensor_tensor(DR[:, 0, 0:T], DN[:, 0, 0:T], c2("cos")[:, NMETA:TA], ALU.mult))
                mark(V.tensor_tensor(DR[:, 1, :], DN[:, 1, :], c2("cos"), ALU.mult))
                dve.wait_ge(d_rot, i + 1)
                mark(V.tensor_tensor(DQK[:, 0, 0:T], AUX[:, 0, 0:T], c2("sin")[:, NMETA:TA], ALU.mult))
                mark(V.tensor_tensor(DQK[:, 1, :], AUX[:, 1, 0:TA], c2("sin"), ALU.mult))
                ch.wait()
                mark(V.tensor_tensor(DQK[:, 0, 0:T], DQK[:, 0, 0:T], DR[:, 0, 0:T], ALU.add))
                V.tensor_tensor(DQK[:, 1, :], DQK[:, 1, :], DR[:, 1, :], ALU.add).then_inc(d_rope, 1)
                dve.wait_ge(b_z, 1 + i)
                take(3, SQF[:], T)
                lo("attn", i, 5)
                take(4, SKF[:], TA)
                dve.wait_ge(d_sc, 1 + i + 1)
                link(V.scalar_tensor_tensor(SS[:], AUX[:, 0:2, 0:q1 + TA], 0.125,
                                            c2("dfmask").unsqueeze(1).broadcast_to([P, 2, q1 + TA]), ALU.mult, ALU.add))
                mark(V.tensor_reduce(ATS[:, 12:14], SS[:, :, 0:q1], AX.X, ALU.max))
                link(V.tensor_reduce(ATS[:, 14:16], SS[:, :, q1:q1 + TA], AX.X, ALU.max))
                V.tensor_scalar(ATS[:, 0:4], ATS[:, 12:16], -1.0, None, ALU.mult).then_inc(d_max, 1)
                lo("attn", i, 6)
                dve.wait_ge(bv_tr, 1 + i)
                take(5, SV[:], TA)
                dve.wait_ge(d_exp, i + 1)
                link(V.reciprocal(ATS[:, 8:12], ATS[:, 4:8]))
                for t in range(2):
                    mark(V.tensor_scalar(ATS[:, 16 + t:17 + t], ATS[:, 9 + 2 * t:10 + 2 * t], SMALL[:, 19:20], None, ALU.mult))
                ch.wait()
                for t, r in enumerate((slice(0, q1), slice(q1, q1 + TA))):
                    mark(V.tensor_scalar(SS[:, 1, r], SS[:, 1, r], ATS[:, 16 + t:17 + t], None, ALU.mult))
                ch.wait()
                for t, r in enumerate((slice(0, q1), slice(q1, q1 + TA))):
                    ins = V.scalar_tensor_tensor(SS[:, 0, r], SS[:, 0, r], ATS[:, 8 + 2 * t:9 + 2 * t], SS[:, 1, r],
                                                 ALU.mult, ALU.subtract)
                ins.then_inc(d_w, 1)
                dve.wait_ge(bv_tr, 1 + i + 1)
                dve.wait_ge(b_av, 1 + i)
                mark(V.tensor_copy(SVT[:, 0:2, :].rearrange("p a d -> p (a d)"), AUX[:, 2, 0:T]))
                V.tensor_copy(SVT[0:NMETA, 2, :], AUX[0:NMETA, 2, T:T + P]).then_inc(svt_ready, 1)
                dve.wait_ge(b_z, 1 + i + 1)
                mark(V.scalar_tensor_tensor(ZS[:], AUX[:, 1, 0:3 * P], sc, c2("sbmask"), ALU.mult, ALU.add))
                V.tensor_scalar(ZM[0:NMETA, :], AUX[0:NMETA, 2, 0:T], sc, None, ALU.mult).then_inc(b_zs, 1)
                lo("attn", i, 7)
                dve.wait_ge(d_wtr, i + 1)
                mark(V.tensor_copy(WTS[:], AUX[:, 3, 0:3 * P]))
                V.tensor_copy(WTM[0:NMETA, :], AUX[0:NMETA, 0, 0:T]).then_inc(d_wt, 1)
                dve.wait_ge(b_ln, i + 1)
                ch.wait()
                dve.wait_ge(b_zs, i + 1)
                mark(V.scalar_tensor_tensor(LZ[:], ZS[:], 0.0, LZ[:], ALU.max, ALU.add))
                V.scalar_tensor_tensor(LM[0:NMETA, :], ZM[0:NMETA, :], 0.0, LM[0:NMETA, :], ALU.max, ALU.add).then_inc(b_sp, 1)
                dve.wait_ge(b_tail, i + 1)
                mark(V.tensor_tensor(AZ[:], ZS[:], AUX[:, 1, 0:3 * P], ALU.subtract))
                V.tensor_tensor(AM[0:NMETA, :], ZM[0:NMETA, :], AUX[0:NMETA, 3, 0:T], ALU.subtract).then_inc(b_arg, 1)
                lo("attn", i, 8)
                dve.wait_ge(d_orstd, i + 1)
                link(V.scalar_tensor_tensor(MT[:], AUX[:, 0, 0:T], SMALL[:, 20:21], RSD[:], ALU.mult, ALU.mult))
                dve.wait_ge(gate_sig, GSIG + 2 * i + 2)
                V.tensor_tensor(GSB[:], ACC[:, 2, 0:T], GSB[:], ALU.mult).then_inc(bank_free, 1)
                V.tensor_tensor(GDF[:], ACC[:, 3, 0:T], GDF[:], ALU.mult).then_inc(bank_free, 1)
                dve.wait_ge(bank_free, unit("attn", i, 8)[0])
                link(V.tensor_tensor(MT[:], MT[:], GDF[:], ALU.mult))
                mixed(1)
                dve.wait_ge(mix_ready, 1 + 2 * i + 1)
                dve.wait_ge(b_av, 1 + i + 1)
                link(V.tensor_tensor(MT[:], AUX[:, 3, 0:T], GSB[:], ALU.mult))
                mixed(0)
            ch.leave(ITERS["attn"], "v_attn")

            def put(i, p):
                done("proj", i, p)
                V.tensor_tensor(OUTS[:, bass.ds(4 * i + p, 1), :].rearrange("p a t -> p (a t)"), ACC[:, p, 0:T], XF[:, bass.ds(4 * i + p, 1), :].rearrange("p a t -> p (a t)"),
                                ALU.add).then_inc(bank_free, 1)

            dve.wait_ge(mix_ready, 1 + 2 * HEADS)
            with dve.Fori(0, ITERS["proj"] - 1) as i:
                for p in range(4):
                    lo("proj", i, p + 1)
                    put(i, p)
            for p in range(4):
                if p < 3:
                    lo("proj", ITERS["proj"] - 1, p + 1)
                put(ITERS["proj"] - 1, p)


def constants():
    n = np.arange(P)
    masks = [np.eye(P)]
    for l in range(LEVELS - 1):
        masks.append((n[:, None] >> (l + 1) == n[None, :] >> (l + 1)) & ((n[:, None] >> l) != (n[None, :] >> l)))
    con1 = np.concatenate([np.eye(P)] + masks, axis=1).astype(np.float32)
    tri = n[:, None] >= n[None, :]
    rot, half = np.zeros((P, P)), 8
    cos, sin = np.ones((P, TA), np.float32), np.zeros((P, TA), np.float32)
    inv = (np.float32(500000.0) ** (-np.arange(0, 2 * half, 2, dtype=np.float32) / np.float32(2 * half))).astype(np.float32)
    ang = (np.arange(TA, dtype=np.float32)[None, :] * inv[:, None]).astype(np.float32)
    for g in (0, 64):
        for d in range(half):
            rot[g + half + d, g + d] = -1.0
            rot[g + d, g + half + d] = 1.0
            for o in (d, half + d):
                cos[g + o], sin[g + o] = np.cos(ang[d]), np.sin(ang[d])
    strict = np.where(n[:, None] < n[None, :], 0.0, NEG)
    sbmask = np.concatenate([strict, np.zeros((P, P)), strict], axis=1)
    pos = np.arange(TA)
    df = [np.where(pos[None, :P + NMETA] <= n[:, None] + NMETA, 0.0, NEG),
          np.where(pos[None, :] <= n[:, None] + NMETA + P, 0.0, NEG)]
    blk = np.kron(np.eye(2), np.full((64, 64), 1.0 / 64))
    con2 = np.concatenate([tri, rot, cos, sin, sbmask] + df + [blk], axis=1).astype(np.float32)
    return con1, con2


def kernel(**inputs):
    import numpy as np
    import concourse.bacc as bacc
    from concourse.bass_utils import run_bass_kernel_spmd

    g = {k: np.asarray(v) for k, v in inputs.items()}

    def blocks(v):
        return np.ascontiguousarray(v.reshape(-1, P).T)

    def units(w):
        k, n = w.shape
        return w.reshape(k // P, P, n // P, P).transpose(2, 1, 0, 3)

    wm, wi = units(g["w_mod"][0]), units(g["w_in"][0])
    pab = np.concatenate([units(g["w_pa"][0]), units(g["w_pb"][0])], axis=2)
    wo, wu = units(g["w_o"][0]), units(g["w_up"][0])
    w2, wo2 = units(g["w_in_2"][0]), units(g["w_out_2"][0])
    order = []
    for j in range(KD):
        order += [wm[j], wm[KD + j]]
    for h in range(HEADS):
        order += [wi[8 + h], wi[16 + h], wi[24 + h], wi[h]]
    for h in range(HEADS):
        for n, b in enumerate((32, 48, 56, 40)):
            order += [wi[b + h], wm[48 + 4 * h + n]]
    for j in range(KD):
        order += [wi[64 + j], wi[80 + j], pab[j], wm[32 + j]]
    for j in range(KD):
        order += [wo[j], wm[80 + j]]
    for j in range(FF):
        order += [wu[j], wu[FF + j]]
    for h in range(HEADS):
        order += [w2[b + h] for b in (32, 40, 48, 0, 8, 16, 24, 56)]
    order += [wo2[j] for j in range(KD)]
    wts = np.stack(order)
    wd = g["w_down"][0].reshape(4, DT, P, KD, P).transpose(3, 0, 2, 1, 4).reshape(4 * KD, P, DT, P)
    lam = np.zeros((P, 4), np.float32)
    for n, name in enumerate(("lambda_q1_2", "lambda_q2_2", "lambda_k1_2", "lambda_k2_2")):
        lam[:64, n] = g[name][0]
    vec = np.concatenate([
        blocks(g["norm1_g"][0]), blocks(g["norm2_g"][0]), blocks(g["final_g"]), blocks(g["norm_w_2"][0]),
        blocks(g["b_mod"][0]), blocks(g["lb_raw"].reshape(-1)), blocks(g["a_norm_g"][0]),
        blocks(g["sconv_w"][0].reshape(-1)), blocks(g["ffn_dw"][0].reshape(-1)), blocks(g["ffn_db"][0]),
        blocks(np.tile(g["q_norm_w_2"][0], 2)), blocks(np.tile(g["k_norm_w_2"][0], 2)), blocks(g["subln_w_2"][0]),
        np.stack([blocks(g["c"][0]), blocks(g["c_ctx"])], axis=2).reshape(P, -1), lam], axis=1)
    con1, con2 = constants()
    arrays = {
        "xct": np.stack([g["x"][0].T, g["ctx"][0].T]), "metat": np.ascontiguousarray(g["meta_2"].T), "vec": vec,
        "con1": con1, "con2": con2, "wts": wts, "wdown": np.ascontiguousarray(wd),
    }
    nc = bacc.Bacc("TRN2", target_bir_lowering=False, num_devices=1)
    args = [nc.dram_tensor(n, a.shape, F32, kind="ExternalInput").ap() for n, a in arrays.items()]
    args.append(nc.dram_tensor("park", (P, KD, T), F32, kind="Internal").ap())
    args.append(nc.dram_tensor("outt", (KD, P, T), F32, kind="ExternalOutput").ap())
    build(nc, *args)
    r = run_bass_kernel_spmd(nc, [arrays], core_ids=[0])
    return np.ascontiguousarray(r.results[0]["outt"].reshape(D, T).T)[None]
```

```python
from contextlib import ExitStack

import numpy as np

import concourse.bass as bass
from concourse import mybir

F32 = mybir.dt.float32
F32R = mybir.dt.float32r
ACT = mybir.ActivationFunctionType
ALU = mybir.AluOpType
AX = mybir.AxisListType

P = 128
D = 2048
KD = D // P
T = 256
HEADS = 8
FF = 5632 // P
NMETA = 16
TA = T + NMETA
GRID = 64
EPS = 1e-6
SUBLN_EPS = 1e-5
LAM_INIT = 0.8 - 0.6
LEVELS = 8
TINY = 2.0 ** -64
NEG = -1e30
DT = 11
DH = 6

PHASES = [
    ("mod1", 8, "mmmm"),
    ("rec", 8, "ssss"),
    ("mix", 8, "smsmsmsm"),
    ("merge", 8, "sssmsssm"),
    ("out", 8, "smsm"),
    ("up", 22, "ssss"),
    ("down", 8, "ssssssss"),
    ("attn", 8, "ssssssss"),
    ("proj", 4, "ssss"),
]
UNIT0, SPLIT0 = {}, {}
_u = _s = 0
for _n, _it, _k in PHASES:
    UNIT0[_n], SPLIT0[_n] = _u, _s
    _u += _it * len(_k)
    _s += _it * _k.count("s")
ITERS = {n: it for n, it, _ in PHASES}
KINDS = {n: k for n, _, k in PHASES}

VCOLS = {}
_o = 0
for _n, _w in [("norm1", KD), ("norm2", KD), ("final", KD), ("norm_2", KD), ("bmod", 6 * KD), ("lb", 32),
               ("anorm", 1), ("sconv", 24), ("dw", 9 * FF), ("db", FF), ("qn", 1), ("kn", 1),
               ("subln", 1), ("c", 2 * KD), ("lam", 4)]:
    VCOLS[_n] = (_o, _w)
    _o += _w
NVEC = _o

CCOLS = {}
_o = 0
for _n, _w in [("ident", P), ("masks", 8 * P)]:
    CCOLS[_n] = (_o, _w)
    _o += _w
NC1 = _o
C2COLS = {}
_o = 0
for _n, _w in [("tri", P), ("rot", P), ("cos", TA), ("sin", TA), ("sbmask", 3 * P), ("dfmask", P + NMETA + TA),
               ("blk64", P)]:
    C2COLS[_n] = (_o, _w)
    _o += _w
NC2 = _o

CHAIN = {"v_mod1": 6, "v_rec": 6, "v_mix": 36, "v_merge": 2, "v_up": 16, "v_attn": 26, "a_mix": 3, "a_attn": 4,
         "v_out": 15, "p_mix": 12, "p_merge": 6, "p_out": 3}


class Chain:

    def __init__(self, eng, sem):
        self.eng, self.sem, self.base, self.n, self.start = eng, sem, 0, 0, 0

    def enter(self, i, per):
        self.per, self.n, self.start = per, 0, self.base + i * per

    def leave(self, iters, name):
        assert self.n == self.per, f"CHAIN {name} {self.n}"
        self.base += iters * self.per
        self.n, self.start = 0, self.base

    def link(self, ins):
        self.n += 1
        ins.then_inc(self.sem, 1)
        self.eng.wait_ge(self.sem, self.start + self.n)

    def mark(self, ins):
        self.n += 1
        ins.then_inc(self.sem, 1)

    def wait(self):
        self.eng.wait_ge(self.sem, self.start + self.n)

    def wait_but_last(self):
        self.eng.wait_ge(self.sem, self.start + self.n - 1)

    def straight(self):
        self.base = self.base + self.n
        self.n, self.start = 0, self.base


def build(nc, xct, metat, vec, con1, con2, wts, wdown, park, outt):
    ctx = ExitStack()
    with ctx:
        base = 16512

        def at(name, kb, shape, dt=F32):
            return nc.alloc_sbuf_tensor_at(name, shape, dt, offset=base + int(kb * 1024))

        def sem(name):
            return ctx.enter_context(nc.semaphore(name))

        RAW = at("raw", 0, [P, 4, 16, P])
        HI = at("hi", 32, [P, 2, 16, P], F32R)
        LO = at("lo", 48, [P, 2, 16, P], F32R)
        HX = at("hx", 64, [P, 4, KD, T], F32R)
        YAB = at("yab", 96, [P, 4, HEADS, T], F32R)
        XC = at("xc", 128, [P, 2, KD, T])
        SQ1 = at("sq1", 160, [P, 2, 4, 2, T])
        SS1 = at("ss1", 186, [P, 2, T])
        RS1 = at("rs1", 176, [P, 2, T])
        N1 = at("n1", 178, [P, 2, T])
        HN1 = at("hn1", 180, [P, 2, T])
        ROW = at("row", 182, [P, 4, P])
        FG = at("fg", 144, [P, 2, HEADS, T])
        VT = at("vt", 160, [P, 2, HEADS * P])
        ST = at("st", 168, [P, 2, HEADS, P])
        QF = at("qf", 176, [P, HEADS, T])
        MRG = at("mrg", 144, [P, 2, KD, T], F32R)
        X1 = at("x1", 128, [P, KD, T])
        SH = at("sh", 96, [P, FF, T], F32R)
        SL = at("sl", 140, [P, FF, T], F32R)
        XF = at("xf", 64, [P, KD, T])
        U2 = at("u2", 96, [P, 2, KD, TA], F32R)
        MIX = at("mix", 130, [P, 2, 2 * HEADS, T], F32R)
        CON2 = at("con2", 162, [P, NC2])
        CON1 = at("con1", 184 + 13.5, [P, NC1])
        cbase = 184 + 13.5 + NC1 / 256
        VEC = at("vec", cbase, [P, NVEC])
        MODV = at("modv", cbase + 2.75, [P, 6 * KD, 2])
        AM1 = at("am1", cbase + 3.5, [P, KD, 2])
        AM2 = at("am2", cbase + 3.625, [P, KD])
        LBV = at("lbv", cbase + 3.6875, [P, 3, 16])
        CS = at("cs", cbase + 3.875, [P, KD, 2])
        ONESR = at("onesr", cbase + 4.0, [P, P])
        SMALL = at("small", cbase + 4.5, [P, 32])
        SG = at("sg", 128, [P, 2, 2, T])
        FC = at("fc", 132, [P, 2, T])
        LC = at("lc", 134, [P, 2, T])
        EXC = at("exc", 136, [P, 2, T])
        KDT = at("kdt", 138, [P, 4, P])
        VS = at("vs", 140, [P, 2, T])
        VCT = at("vct", 142, [P, 2, P])
        SGQ = at("sgq", 143, [P, T])
        ONE = at("one", 184, [P, T])
        AR = at("ar", 128, [P, 4, T])
        TT0 = at("tt0", 132, [P, 3, T])
        QK1 = at("qk1", 135, [P, 2, T])
        QK0 = at("qk0", 137, [P, 2, T])
        QL = at("ql", 139, [P, 2, 2, T])
        KS = at("ks", 143, [P, T])
        TT1 = at("tt1", 184, [P, 3, P])
        SCT = at("sct", 185.5, [P, 2, 4, P])
        SC = at("sc", 189.5, [P, 2, T])
        QS = at("qs", 191.5, [P, 2, T])
        GS = at("gs", 193.5, [P, T])
        SGG = at("sgg", 194.5, [P, T])
        UP = at("up", 195.5, [P, T + 8])
        ON = at("on", 185.5, [P, 2, P])
        OSQ = at("osq", 186.5, [P, 2, P])
        YT = at("yt", 187.5, [P, T])
        SCB = at("scb", cbase + 4.625, [P, T])
        GA = at("ga", 184, [P, T])
        GB = at("gb", 185, [P, T])
        M1 = at("m1", 186, [P, T])
        M2 = at("m2", 187, [P, T])
        SQ2 = at("sq2", 184, [P, 2, T])
        ZERO = at("zero", 196.25, [P, T])
        RS2 = at("rs2", 187, [P, T])
        N2 = at("n2", 188, [P, 8, T])
        AT = at("at", 184, [P, 6, GRID + 2])
        CV = at("cv", 185.75, [P, T])
        CV2 = at("cv2", 186.75, [P, T])
        S1 = at("s1", 187.75, [P, T])
        SQ3 = at("sq3", 192, [P, 2, 2, T])
        RSF = at("rsf", 190, [P, T])
        MSF = at("msf", 191, [P, T])
        METT = at("mett", 80, [P, KD, NMETA])
        RS3 = at("rs3", 81, [P, TA])
        SQM = at("sqm", 82.0625, [P, KD, NMETA])
        N3 = at("n3", 84.1875, [P, 4, TA])
        a0 = 80

        DQK = at("dqk", a0, [P, 2, TA])
        DN = at("dn", a0 + 2.125, [P, 2, TA])
        DR = at("dr", a0 + 4.25, [P, 2, TA])
        DV = at("dv", a0 + 6.375, [P, TA])
        DVT = at("dvt", a0 + 7.4375, [P, 3, P])
        SV = at("sv", a0 + 8.9375, [P, TA])
        SVT = at("svt", a0 + 10, [P, 3, P])
        SQF = at("sqf", a0 + 11.5, [P, T])
        SKF = at("skf", a0 + 12.5, [P, TA])
        GSB = at("gsb", a0 + 13.5625, [P, T])
        GDF = at("gdf", a0 + 14.5625, [P, T])
        b0 = 162 + NC2 / 256
        SS = at("ss", b0, [P, 2, P + NMETA + TA])
        WTS = at("wts", b0 + 3.25, [P, 3 * P])
        WTM = at("wtm", b0 + 4.75, [P, T])
        ZS = at("zs", b0 + 5.75, [P, 3 * P])
        ZM = at("zm", b0 + 7.25, [P, T])
        LZ = at("lz", b0 + 8.25, [P, 3 * P])
        LM = at("lm", b0 + 9.75, [P, T])
        AZ = at("az", b0 + 10.75, [P, 3 * P])
        AM = at("am", b0 + 12.25, [P, T])
        MT = at("mt", b0 + 13.25, [P, T])
        OD = at("od", b0 + 14.25, [P, T])
        RSD = at("rsd", b0 + 15.25, [P, T])
        SGA = at("sga", b0 + 16.25, [P, T])
        ONEP = at("onep", b0 + 17.25, [P, P])
        ON128 = at("on128", b0 + 17.75, [P, P])
        ATS = at("ats", b0 + 18.25, [P, 24])
        OUTS = at("outs", 80, [P, KD, T])

        ACC = ctx.enter_context(nc.psum_tensor("acc", [P, 4, 512], F32))
        AUX = ctx.enter_context(nc.psum_tensor("aux", [P, 4, 512], F32))

        raw_full = [sem(f"raw_full{i}") for i in range(4)]
        hi_half, lo_half = sem("hi_half"), sem("lo_half")
        mm_half = sem("mm_half")
        bank_free = sem("bank_free")
        v_chain, a_chain = sem("v_chain"), sem("a_chain")
        in_vec, in_con, in_x, in_con2, in_meta = (sem(n) for n in ("in_vec", "in_con", "in_x", "in_con2", "in_meta"))
        c_sig, c_silu, ones_set = sem("c_sig"), sem("c_silu"), sem("ones_set")
        mod_sum, p_chain = sem("mod_sum"), sem("p_chain")
        mod_sum_v = sem("mod_sum_v")
        col_mm = sem("col_mm")
        lb_exp, lb_max = sem("lb_exp"), sem("lb_max")
        sq1_done, sq1_read, ss1_mm, rs1_done = sem("sq1_done"), sem("sq1_read"), sem("ss1_mm"), sem("rs1_done")
        n1_ready, h1_aff, hx_ready = sem("n1_ready"), sem("h1_aff"), sem("hx_ready")
        gate_sig = sem("gate_sig")
        ctx_f, ctx_ln, ctx_scan, ctx_exp, kd_ready = (sem(n) for n in ("ctx_f", "ctx_ln", "ctx_scan", "ctx_exp", "kd_ready"))
        kd_tr, kdt_ready, v_tr, vt_ready, s_mm, s_ready = (
            sem(n) for n in ("kd_tr", "kdt_ready", "v_tr", "vt_ready", "s_mm", "s_ready"))
        f_ready, f_ln, lv_sum, lv_exp, lv_mul, ks_ready = (
            sem(n) for n in ("f_ready", "f_ln", "lv_sum", "lv_exp", "lv_mul", "ks_ready"))
        sc_mm, sc_read, o_mm, o_rstd, on_ready, on_tr, ya_ready = (
            sem(n) for n in ("sc_mm", "sc_read", "o_mm", "o_rstd", "on_ready", "on_tr", "ya_ready"))
        yb_ready, mrg_ready = sem("yb_ready"), sem("mrg_ready")
        in_x1, x1_chunk, sq2_done, ss2_mm, rs2_done, n2_ready, h2_aff, hx2_ready, x1_out, zero_set = (
            sem(n) for n in ("in_x1", "x1_chunk", "sq2_done", "ss2_mm", "rs2_done", "n2_ready", "h2_aff",
                             "hx2_ready", "x1_out", "zero_set"))
        a_copied, cv_ready, cv_sig, s_hidden = sem("a_copied"), sem("cv_ready"), sem("cv_sig"), sem("s_hidden")
        in_x1b, x2_chunk, sq3_done, ss3_mm, rs3_done = (
            sem(n) for n in ("in_x1b", "x2_chunk", "sq3_done", "ss3_mm", "rs3_done"))
        xf_ready, sqm_done, ssm_mm, ms4_done, rs4_done, u2_ready = (
            sem(n) for n in ("xf_ready", "sqm_done", "ssm_mm", "ms4_done", "rs4_done", "u2_ready"))
        at_const, lam_mm, lam_exp, lam_ready, lam_prod = (
            sem(n) for n in ("at_const", "lam_mm", "lam_exp", "lam_ready", "lam_prod"))
        d_sq, d_ms, d_rstd, d_norm, d_rot, d_rope, dv_tr, dvt_ready = (
            sem(n) for n in ("d_sq", "d_ms", "d_rstd", "d_norm", "d_rot", "d_rope", "dv_tr", "dvt_ready"))
        d_sc, d_max, d_exp, d_w, d_wtr, d_wt, d_av, d_osq, d_oms, d_orstd = (
            sem(n) for n in ("d_sc", "d_max", "d_exp", "d_w", "d_wtr", "d_wt", "d_av", "d_osq", "d_oms", "d_orstd"))
        b_v, bv_tr, svt_ready, b_z, b_zs, b_ln, b_sp, b_tail, b_arg, b_a, b_av = (
            sem(n) for n in ("b_v", "bv_tr", "svt_ready", "b_z", "b_zs", "b_ln", "b_sp", "b_tail", "b_arg", "b_a", "b_av"))
        mix_ready = sem("mix_ready")
        out_done = sem("out_done")

        def vc(name, j=0, n=1):
            o = VCOLS[name][0] + j
            return VEC[:, o:o + n]

        def vcd(name, j):
            return VEC[:, bass.ds(VCOLS[name][0] + j, 1)]

        def c1(name):
            o, w = CCOLS[name]
            return CON1[:, o:o + w]

        def c2(name):
            o, w = C2COLS[name]
            return CON2[:, o:o + w]

        def unit(ph, i, p):
            L = len(KINDS[ph])
            return UNIT0[ph] + i * L + p, UNIT0[ph] // 4 + i * (L // 4) + p // 4

        def split(ph, i, p):
            k = KINDS[ph]
            n = (k + "s")[:p].count("s")
            return SPLIT0[ph] + i * k.count("s") + n, n % 2

        def slot_distance(ph, p):
            return {"mix": 3, "out": 3, "merge": (3, 3, 2)[p % 4] if p % 4 < 3 else 0}.get(ph, 2)

        def halves(ph):
            return ((0, DH), (DH, DT)) if ph == "down" else ((0, 8), (8, 16))

        block = ctx.enter_context(nc.Block())

        @block.sync
        def _(sp):
            def load(ph, i, p, first=False):
                u, u4 = unit(ph, i, p)
                back = {"mix": {0: 2, 2: 2, 4: 2, 6: 2}, "merge": {0: 2, 2: 3, 4: 3, 5: 3, 6: 3}, "out": {0: 2, 2: 2}}.get(ph, {})
                if p in back:
                    s = split(ph, i, p)[0]
                    sp.wait_ge(lo_half, 2 * (s - back[p]) + 2)
                elif not first:
                    sp.wait_ge(mm_half, 2 * (u - 3))
                if ph == "down":
                    src = wdown[bass.ds(u - UNIT0[ph], 1)].rearrange("a p t n -> (a p) t n")
                    sp.dma_start(RAW[:, p % 4, 0:DT, :], src).then_inc(raw_full[p % 4], 16)
                else:
                    w = u if UNIT0[ph] < UNIT0["down"] else u - 64
                    src = wts[bass.ds(w, 1)].rearrange("a p t n -> (a p) t n")
                    sp.dma_start(RAW[:, p % 4, :, :], src).then_inc(raw_full[p % 4], 16)

            sp.dma_start(VEC[:], vec).then_inc(in_vec, 16)
            sp.dma_start(CON1[:], con1).then_inc(in_con, 16)
            for p in range(4):
                load("mod1", 0, p, True)
            sp.dma_start(XC[:], xct.rearrange("s (k p) t -> p s k t", p=P)).then_inc(in_x, 16)
            with sp.Fori(1, ITERS["mod1"]) as i:
                for p in range(4):
                    load("mod1", i, p)
            for ph, iters, kinds in PHASES[1:4]:
                with sp.Fori(0, iters) as i:
                    for p in range(len(kinds)):
                        load(ph, i, p)
            sp.wait_ge(ya_ready, 1 + HEADS)
            sp.dma_start(X1[:], xct[0].rearrange("(k p) t -> p k t", p=P)).then_inc(in_x1, 16)
            with sp.Fori(0, ITERS["out"]) as i:
                for p in range(4):
                    load("out", i, p)
            with sp.Fori(0, ITERS["up"]) as i:
                for p in range(4):
                    load("up", i, p)
            with sp.Fori(0, ITERS["down"]) as i:
                for p in range(8):
                    load("down", i, p)
            with sp.Fori(0, ITERS["attn"]) as i:
                for p in range(8):
                    load("attn", i, p)
            with sp.Fori(0, ITERS["proj"]) as i:
                for p in range(4):
                    load("proj", i, p)

        def pool_units(ph, i):
            if ph == "mix":
                return [(p, 4 * i + p // 2) for p in (1, 3, 5, 7)]
            if ph == "merge":
                return [(p, 4 * HEADS + 2 * i + p // 4) for p in (3, 7)]
            return [(1, 4 * HEADS + KD + i)]

        @block.gpsimd
        def _(pool):
            ch = Chain(pool, p_chain)

            pool.wait_ge(c_silu, 1)
            for ph in ("mix", "merge", "out"):
                with pool.Fori(0, ITERS[ph]) as i:
                    ch.enter(i, CHAIN["p_" + ph])
                    for p, _ in pool_units(ph, i):
                        pool.wait_ge(raw_full[p % 4], 16 * (unit(ph, i, p)[1] + 1))
                        w = RAW[:, p % 4]
                        ch.link(nc.gpsimd.tensor_tensor(w, w, CS[:, :, 0].unsqueeze(2).broadcast_to([P, KD, P]), ALU.mult))
                        for n in (8, 4, 2):
                            ins = nc.gpsimd.tensor_tensor(w[:, 0:n, :], w[:, 0:n, :], w[:, n:2 * n, :], ALU.add)
                            if n > 2:
                                ch.link(ins)
                        ins.then_inc(mod_sum, 1)
                ch.leave(ITERS[ph], "p_" + ph)
            pool.wait_ge(bank_free, UNIT0["up"])
            pool.dma_start(park, X1[:]).then_inc(x1_out, 16)
            pool.wait_ge(x1_out, 16)
            pool.wait_ge(mm_half, 2 * UNIT0["down"])
            pool.dma_start(XF[:], park).then_inc(in_x1b, 16)
            pool.dma_start(METT[:], metat.rearrange("(k p) t -> p k t", p=P)).then_inc(in_meta, 16)
            pool.wait_ge(mm_half, 2 * UNIT0["attn"])
            pool.dma_start(CON2[:], con2).then_inc(in_con2, 16)
            with pool.Fori(0, ITERS["proj"]) as i:
                for p in range(4):
                    pool.wait_ge(bank_free, unit("proj", i, p)[0] + 1)
                    dst = outt[bass.ds(4 * i + p, 1)].rearrange("a p t -> (a p) t")
                    pool.dma_start(dst, OUTS[:, bass.ds(4 * i + p, 1), :].rearrange("p a t -> p (a t)")).then_inc(out_done, 16)
            pool.wait_ge(x1_out, 16)
            pool.wait_ge(out_done, 16 * KD)

        @block.scalar
        def _(act):
            A = nc.scalar
            for one in (kdt_ready, s_ready, lv_exp, h1_aff, cv_sig, sq2_done, sq3_done):
                act.sem_inc(one, 1)
            ch = Chain(act, a_chain)

            def hi(ph, i, p):
                L = len(KINDS[ph])
                if p < L and KINDS[ph][p] == "m":
                    return
                u, u4 = unit(ph, i, p)
                s, slot = split(ph, i, p)
                act.wait_ge(raw_full[p % 4], 16 * (u4 + 1))
                for h, (a, b) in enumerate(halves(ph) if p < L else ((0, 8), (8, 16))):
                    need = 2 if ph == "down" and p == L else h + 1
                    act.wait_ge(mm_half, 2 * (u - slot_distance(ph, p)) + need)
                    A.activation(HI[:, slot, a:b, :], RAW[:, p % 4, a:b, :], ACT.Copy).then_inc(hi_half, 1)

            def done(ph, i, p):
                act.wait_ge(mm_half, 2 * unit(ph, i, p)[0] + 2)

            act.wait_ge(in_vec, 16)
            A.activation(CS[:], VEC[:, VCOLS["c"][0]:VCOLS["c"][0] + 2 * KD].rearrange("p (k s) -> p k s", s=2),
                         ACT.Sigmoid).then_inc(c_sig, 1)
            act.wait_ge(lb_max, 1)
            A.activation(LBV[:, 0:2, :], LBV[:, 0:2, :], ACT.Exp).then_inc(lb_exp, 1)
            act.wait_ge(in_x, 16)
            for g in range(4):
                if g >= 2:
                    act.wait_ge(sq1_read, g - 1)
                for s in range(2):
                    ins = A.activation(SQ1[:, g % 2, :, s, :], XC[:, s, 4 * g:4 * g + 4, :], ACT.Square)
                ins.then_inc(sq1_done, 1)
            act.wait_ge(ss1_mm, 1)
            act.wait_ge(ones_set, 1)
            ch.link(A.activation(RS1[:].rearrange("p s t -> p (s t)"), AUX[:, 0, :], ACT.Ln, bias=SMALL[:, 0:1]))
            A.activation(RS1[:], RS1[:], ACT.Exp, scale=-0.5).then_inc(rs1_done, 1)
            ch.straight()
            with act.Fori(0, ITERS["mod1"]) as i:
                for p in (0, 1):
                    j = 2 * i + p
                    act.wait_ge(n1_ready, j + 1)
                    for s in range(2):
                        ins = A.activation(HN1[:, s, :], N1[:, s, :], ACT.Identity,
                                           bias=MODV[:, bass.ds(j, 1), s:s + 1].rearrange("p a b -> p (a b)"),
                                           scale=AM1[:, bass.ds(j, 1), s:s + 1].rearrange("p a b -> p (a b)"))
                    ins.then_inc(h1_aff, 1)
            hi("rec", 0, 0)

            with act.Fori(0, ITERS["rec"]) as i:
                for d in (0, 1):
                    hi("rec", i, d + 1)
                    done("rec", i, d)
                    act.wait_ge(bank_free, unit("rec", i, d)[0] - 3)
                    A.activation(SG[:, d].rearrange("p s t -> p (s t)"), ACC[:, d, :], ACT.Sigmoid).then_inc(gate_sig, 1)
                hi("rec", i, 3)
                act.wait_ge(ctx_f, i + 1)
                A.activation(LC[:], LC[:], ACT.Ln).then_inc(ctx_ln, 1)
                act.wait_ge(ctx_scan, i + 1)
                A.activation(EXC[:], EXC[:], ACT.Exp).then_inc(ctx_exp, 1)
                act.wait_ge(kd_tr, 1 + i + 1)
                A.activation(KDT[:].rearrange("p a b -> p (a b)"), AUX[:, 0, :], ACT.Copy).then_inc(kdt_ready, 1)
                hi("rec", i, 4)
                done("rec", i, 3)
                act.wait_ge(bank_free, unit("rec", i, 0)[0])
                A.activation(SGQ[:], ACC[:, 3, 0:T], ACT.Sigmoid).then_inc(gate_sig, 1)
                act.wait_ge(s_mm, 1 + i + 1)
                A.activation(ST[:, :, bass.ds(i, 1), :].rearrange("p s a d -> p s (a d)"),
                             AUX[:, 2, 0:2 * P].rearrange("p (s d) -> p s d", s=2), ACT.Copy).then_inc(s_ready, 1)

            GSIG = 3 * HEADS

            def mix_norm(i):
                act.wait_ge(o_mm, 1 + i + 1)
                for t in range(2):
                    ins = A.activation(OSQ[:, t, :], AUX[:, 3, t * P:(t + 1) * P], ACT.Square,
                                       accum_out=SMALL[:, 4 + t:5 + t])
                ch.link(ins)
                ch.link(A.activation(SMALL[:, 6:8], SMALL[:, 4:6], ACT.Ln, scale=1.0 / P, bias=SMALL[:, 0:1]))
                ch.link(A.activation(SMALL[:, 8:10], SMALL[:, 6:8], ACT.Exp, scale=-0.5))
                A.activation(SMALL[:, 10:12], SMALL[:, 8:10], ACT.Copy).then_inc(o_rstd, 1)

            def mix_head(i, peeled):
                def level(l):
                    h = 1 << l
                    act.wait_ge(lv_sum, 9 * i + l + 1)
                    act.wait_ge(sc_mm, 1 + 9 * i + (l if l >= 2 else 0))
                    q = QL[:, l % 2].rearrange("p a (n two h) -> p a n two h", two=2, h=h)
                    r = AR[:].rearrange("p a (n two h) -> p a n two h", two=2, h=h)
                    for side, src in ((1, 0), (0, 2)):
                        ins = A.activation(q[:, :, :, side, :], r[:, src:src + 2, :, side, :], ACT.Exp)
                    ins.then_inc(lv_exp, 1)

                act.wait_ge(f_ready, i + 1)
                act.wait_ge(lv_exp, 1 + 9 * i)
                A.activation(AR[:, 0:3:2, :], TT0[:, 0:2, :], ACT.Ln).then_inc(f_ln, 1)
                level(0)
                hi("mix", i, 2)
                level(1)
                if not peeled:
                    mix_norm(i - 1)
                level(2)
                hi("mix", i, 4)
                done("mix", i, 0)
                act.wait_ge(bank_free, unit("mix", i, 0)[0] - 1)
                A.activation(SGG[:], ACC[:, 0, 0:T], ACT.Sigmoid).then_inc(gate_sig, 1)
                level(3)
                hi("mix", i, 6)
                level(4)
                level(5)
                hi("mix", i, 8)
                level(6)
                level(7)
                act.wait_ge(lv_sum, 9 * i + 9)
                for d in range(2):
                    ins = A.activation(QS[:, d, :], AR[:, 2 * d, :], ACT.Exp)
                ins.then_inc(lv_exp, 1)

            mix_head(0, True)
            with act.Fori(1, ITERS["mix"]) as i:
                ch.enter(i - 1, CHAIN["a_mix"])
                mix_head(i, False)
            ch.leave(ITERS["mix"] - 1, "a_mix")
            mix_norm(HEADS - 1)
            ch.straight()

            act.wait_ge(ya_ready, 1 + HEADS)
            act.wait_ge(yb_ready, HEADS)
            with act.Fori(0, ITERS["merge"]) as i:
                for jj in range(2):
                    p = 4 * jj
                    hi("merge", i, p + 1)
                    done("merge", i, p)
                    act.wait_ge(bank_free, unit("merge", i, p)[0] - 1)
                    A.activation(GA[:], ACC[:, 0, 0:T], ACT.Sigmoid).then_inc(gate_sig, 1)
                    hi("merge", i, p + 2)
                    done("merge", i, p + 1)
                    A.activation(GB[:], ACC[:, 1, 0:T], ACT.Sigmoid).then_inc(gate_sig, 1)
                    hi("merge", i, p + 4)

            with act.Fori(0, ITERS["out"]) as i:
                for jj in range(2):
                    hi("out", i, 2 * jj + 2)
                    act.wait_ge(bank_free, unit("out", i, 2 * jj)[0] + 1)
                    act.wait_ge(ss2_mm, 1 + 2 * i + jj)
                    A.activation(SQ2[:, jj, :], X1[:, bass.ds(2 * i + jj, 1), :].rearrange("p a t -> p (a t)"),
                                 ACT.Square).then_inc(sq2_done, 1)
            act.wait_ge(ss2_mm, 1 + KD + 1)
            ch.link(A.activation(RS2[:], AUX[:, 0, 0:T], ACT.Ln, bias=SMALL[:, 0:1]))
            A.activation(RS2[:], RS2[:], ACT.Exp, scale=-0.5).then_inc(rs2_done, 1)
            ch.straight()
            for g in range(4):
                act.wait_ge(n2_ready, g + 1)
                for k in range(4):
                    j = 4 * g + k
                    ins = A.activation(N2[:, 4 * (g % 2) + k, :], N2[:, 4 * (g % 2) + k, :], ACT.Identity, bias=MODV[:, 48 + j, 0:1],
                                       scale=AM2[:, j:j + 1])
                ins.then_inc(h2_aff, 1)

            with act.Fori(0, ITERS["up"]) as i:
                for jj in range(2):
                    hi("up", i, 2 * jj + 1)
                    done("up", i, 2 * jj)
                    act.wait_ge(cv_ready, 1 + 2 * i + jj)
                    act.wait_ge(cv_sig, 1 + 2 * i + jj)
                    j = 2 * i + jj
                    A.activation(AT[:, 1:5, 1:GRID + 1], ACC[:, 2 * jj, 0:T].rearrange("p (r c) -> p r c", c=GRID), ACT.Copy)
                    A.activation(CV[:], ACC[:, 2 * jj, 0:T], ACT.Identity, scale=vcd("dw", 4 * FF + j),
                                 bias=vcd("db", j)).then_inc(a_copied, 1)
                    hi("up", i, 2 * jj + 2)
                    act.wait_ge(cv_ready, 1 + 2 * i + jj + 1)
                    act.wait_ge(s_hidden, 1 + j)
                    A.activation(S1[:], CV[:], ACT.Silu).then_inc(cv_sig, 1)

            with act.Fori(0, ITERS["down"]) as i:
                for jj in range(2):
                    for q in range(4):
                        hi("down", i, 4 * jj + q + 1)
                    act.wait_ge(bank_free, unit("down", i, 4 * jj + 3)[0] + 1)
                    act.wait_ge(ss3_mm, 1 + 2 * i + jj)
                    x = XF[:, bass.ds(2 * i + jj, 1), :].rearrange("p a t -> p (a t)")
                    A.activation(SQ3[:, jj, 0, :], x, ACT.Square)
                    A.activation(SQ3[:, jj, 1, :], x, ACT.Square, scale=vcd("final", 2 * i + jj)).then_inc(sq3_done, 1)
            act.wait_ge(in_meta, 16)
            A.activation(SQM[:], METT[:], ACT.Square).then_inc(sqm_done, 1)
            act.wait_ge(ss3_mm, 1 + KD + 1)
            ch.link(A.activation(RSF[:], AUX[:, 0, 0:T], ACT.Ln, bias=SMALL[:, 0:1]))
            A.activation(RSF[:], RSF[:], ACT.Exp, scale=-0.5).then_inc(rs3_done, 1)
            act.wait_ge(ssm_mm, 1)
            A.activation(RS3[:, 0:NMETA], AUX[:, 2, 0:NMETA], ACT.Ln, bias=SMALL[:, 0:1])
            act.wait_ge(ms4_done, 1)
            ch.link(A.activation(RS3[:, NMETA:TA], MSF[:], ACT.Ln, bias=SMALL[:, 0:1]))
            A.activation(RS3[:], RS3[:], ACT.Exp, scale=-0.5).then_inc(rs4_done, 1)
            ch.straight()
            act.wait_ge(lam_mm, 1)
            A.activation(SMALL[:, 16:18], AUX[:, 3, 0:2], ACT.Exp).then_inc(lam_exp, 1)

            GSIG = GSIG + HEADS + 2 * KD
            with act.Fori(0, ITERS["attn"]) as i:
                ch.enter(i, CHAIN["a_attn"])
                hi("attn", i, 1)
                hi("attn", i, 2)
                act.wait_ge(d_sq, i + 1)
                hi("attn", i, 3)
                act.wait_ge(d_ms, i + 1)
                A.activation(DR[:, 0, 0:T], AUX[:, 0, 0:T], ACT.Ln, bias=SMALL[:, 0:1])
                ch.link(A.activation(DR[:, 1, :], AUX[:, 1, 0:TA], ACT.Ln, bias=SMALL[:, 0:1]))
                A.activation(DR[:, 0, 0:T], DR[:, 0, 0:T], ACT.Exp, scale=-0.5)
                A.activation(DR[:, 1, :], DR[:, 1, :], ACT.Exp, scale=-0.5).then_inc(d_rstd, 1)
                hi("attn", i, 4)
                hi("attn", i, 5)
                act.wait_ge(d_max, i + 1)
                for c in range(2):
                    for t, (a, b) in enumerate(((0, P + NMETA), (P + NMETA, P + NMETA + TA))):
                        ins = A.activation(SS[:, c, a:b], SS[:, c, a:b], ACT.Exp,
                                           bias=ATS[:, 2 * t + c:2 * t + c + 1],
                                           accum_out=ATS[:, 4 + 2 * t + c:5 + 2 * t + c])
                ins.then_inc(d_exp, 1)
                hi("attn", i, 6)
                hi("attn", i, 7)
                act.wait_ge(b_zs, i + 1)
                A.activation(LZ[:], ZS[:], ACT.Abs)
                ch.link(A.activation(LM[0:NMETA, :], ZM[0:NMETA, :], ACT.Abs))
                A.activation(LZ[:], LZ[:], ACT.Exp, scale=-1.0)
                ch.link(A.activation(LM[0:NMETA, :], LM[0:NMETA, :], ACT.Exp, scale=-1.0))
                A.activation(LZ[:], LZ[:], ACT.Ln, bias=SMALL[:, 1:2])
                A.activation(LM[0:NMETA, :], LM[0:NMETA, :], ACT.Ln, bias=SMALL[0:NMETA, 1:2]).then_inc(b_ln, 1)
                act.wait_ge(d_av, 1 + i + 1)
                A.activation(OD[:], AUX[:, 0, 0:T], ACT.Square).then_inc(d_osq, 1)
                act.wait_ge(d_oms, i + 1)
                ch.link(A.activation(RSD[:], AUX[:, 2, 0:T], ACT.Ln, bias=SMALL[:, 2:3]))
                A.activation(RSD[:], RSD[:], ACT.Exp, scale=-0.5).then_inc(d_orstd, 1)
                hi("attn", i, 8)
                act.wait_ge(b_arg, i + 1)
                A.activation(AZ[:], AZ[:], ACT.Exp)
                A.activation(AM[0:NMETA, :], AM[0:NMETA, :], ACT.Exp).then_inc(b_a, 1)
                for g, p in ((0, 6), (1, 7)):
                    done("attn", i, p)
                    A.activation((GSB, GDF)[g][:], ACC[:, p % 4, 0:T], ACT.Sigmoid).then_inc(gate_sig, 1)
            ch.leave(ITERS["attn"], "a_attn")

            with act.Fori(0, ITERS["proj"] - 1) as i:
                for p in range(4):
                    hi("proj", i, p + 1)
            for p in range(3):
                hi("proj", ITERS["proj"] - 1, p + 1)

        @block.tensor
        def _(pe):
            for one in (kd_tr, v_tr, s_mm, sc_mm, o_mm, ss2_mm, ss3_mm, d_sc, dv_tr, d_av, b_z, bv_tr, b_av):
                pe.sem_inc(one, 1)
            def mm(*a, **k):
                return pe.matmul(*a, **k)

            def mod_rest(ph, i, p):
                u = unit(ph, i, p)[0]
                if (ph, p) == ("out", 3):
                    pe.wait_ge(mod_sum_v, i + 1)
                else:
                    pe.wait_ge(mod_sum, dict(pool_units(ph, i))[p] + 1)
                pe.wait_ge(bank_free, u - 3)
                for k in range(2):
                    ins = mm(ACC[:, p % 4, 0:1], RAW[:, p % 4, k, :], SMALL[:, 3:4], start=k == 0, stop=k == 1)
                ins.then_inc(mm_half, 2)

            def prod(ph, i, p, xh, xl, out, groups=None, bank_wait=None, between=None,
                     inputs=None):
                u, _ = unit(ph, i, p)
                s, slot = split(ph, i, p)
                if bank_wait is None:
                    pe.wait_ge(bank_free, u - 3)
                elif bank_wait is not False:
                    pe.wait_ge(bank_free, bank_wait)
                n = halves(ph)[1][1]
                for h, (a, b) in enumerate(halves(ph)):
                    if h and between:
                        between()
                    pe.wait_ge(lo_half, 2 * s + h + 1)
                    for k in range(a, b):
                        if inputs and k % 4 == 0:
                            pe.wait_ge(inputs, k // 4 + 1)
                        first, last = groups(k) if groups else (k == 0, k == n - 1)
                        o = out(k)
                        mm(o, HI[:, slot, k, :], xh(k), start=first, stop=False)
                        mm(o, HI[:, slot, k, :], xl(k), start=False, stop=False)
                        ins = mm(o, LO[:, slot, k, :], xh(k), start=False, stop=last)
                    ins.then_inc(mm_half, 1)

            def turn(i, p):
                pe.wait_ge(bank_free, unit("mod1", i, p)[0] + 1)
                mm(AUX[:, (p + 1) % 4, 0:2], ROW[0:2, p, :], c1("ident")[0:2, 0:2], start=True, stop=True).then_inc(col_mm, 1)

            def rows(i, p, first=False):
                u, u4 = unit("mod1", i, p)
                pe.wait_ge(raw_full[p], 16 * (u4 + 1))
                if not first:
                    pe.wait_ge(bank_free, u - 3)
                for k in range(KD):
                    ins = mm(ACC[0:2, p, 0:P], CS[:, k, :], RAW[:, p, k, :], start=k == 0, stop=k == KD - 1)
                ins.then_inc(mm_half, 2)

            pe.wait_ge(c_silu, 1)
            for p in range(4):
                rows(0, p, True)
            pe.wait_ge(in_con, 16)
            for p in range(3):
                turn(0, p)
            rows(1, 0)
            rows(1, 1)
            pe.wait_ge(sq1_read, 4)
            mm(AUX[:, 0, :], ONESR[:], SS1[:].rearrange("p s t -> p (s t)"), start=True, stop=True).then_inc(ss1_mm, 1)
            rows(1, 2)
            pe.wait_ge(rs1_done, 1)
            turn(0, 3)
            turn(1, 0)
            turn(1, 1)
            rows(1, 3)
            turn(1, 2)
            turn(1, 3)
            with pe.Fori(2, ITERS["mod1"]) as i:
                for p in range(4):
                    rows(i, p)
                    if p > 0:
                        turn(i, p - 1)
                turn(i, 3)

            pe.wait_ge(hx_ready, KD)
            with pe.Fori(0, ITERS["rec"]) as i:
                xch, xcl = (lambda k: HX[:, 0:3:2, k, :]), (lambda k: HX[:, 1:4:2, k, :])
                for p in range(3):
                    prod("rec", i, p, xch, xcl, lambda k: ACC[:, p, :].rearrange("p (s t) -> p s t", s=2))

                def turns():
                    pe.wait_ge(kd_ready, i + 1)
                    pe.wait_ge(kdt_ready, 1 + i)
                    for d in range(2):
                        for t in range(2):
                            ins = pe.transpose(AUX[:, 0, (2 * d + t) * P:(2 * d + t + 1) * P], EXC[:, d, t * P:(t + 1) * P], c1("ident"))
                    ins.then_inc(kd_tr, 1)
                    pe.wait_ge(bank_free, unit("rec", i, 2)[0] + 1)
                    pe.wait_ge(vt_ready, 1 + i)
                    for s in range(2):
                        for t in range(2):
                            ins = pe.transpose(AUX[:, 1, (2 * s + t) * P:(2 * s + t + 1) * P], VS[:, s, t * P:(t + 1) * P], c1("ident"))
                    ins.then_inc(v_tr, 1)

                prod("rec", i, 3, lambda k: HX[:, 0, k, :], lambda k: HX[:, 1, k, :], lambda k: ACC[:, 3, 0:T],
                     between=turns)
                pe.wait_ge(kdt_ready, 1 + i + 1)
                pe.wait_ge(vt_ready, 1 + i + 1)
                pe.wait_ge(s_ready, 1 + i)
                for d in range(2):
                    for t in range(2):
                        ins = mm(AUX[:, 2, d * P:(d + 1) * P], KDT[:, 2 * d + t, :], VCT[:, t, :], start=t == 0, stop=t == 1)
                ins.then_inc(s_mm, 1)

            pe.wait_ge(s_ready, 1 + HEADS)

            def mix_cross(i):
                pe.wait_ge(lv_mul, 9 * i + 8)
                pe.wait_ge(ya_ready, 1 + i)
                mm(AUX[:, 2, 0:P], QL[:, 1, 1, 0:P], QL[:, 1, 0, P:T], start=True, stop=True)
                mm(AUX[:, 2, P:T], QL[:, 1, 1, P:T], QL[:, 1, 0, 0:P], start=True, stop=True).then_inc(sc_mm, 1)

            def mix_outputs(i):
                pe.wait_ge(sc_read, 1 + 3 * i + 3)
                pe.wait_ge(lv_mul, 9 * i + 9)
                for t in range(2):
                    o = AUX[:, 3, t * P:(t + 1) * P]
                    for s in range(2):
                        mm(o, SC[:, s, t * P:(t + 1) * P], VT[:, s, bass.ds(i * P, P)], start=s == 0, stop=False)
                    for d in range(2):
                        ins = mm(o, QS[:, d, t * P:(t + 1) * P], ST[:, d, bass.ds(i, 1), :].rearrange("p a d -> p (a d)"),
                                 start=False, stop=d == 1)
                ins.then_inc(o_mm, 1)

            def mix_turn(i):
                pe.wait_ge(on_ready, i + 1)
                for t in range(2):
                    ins = pe.transpose(AUX[:, 2, T + t * P:T + (t + 1) * P], ON[:, t, :], c1("ident"))
                ins.then_inc(on_tr, 1)

            def mix_head(i, peeled):
                xh, xl = (lambda k: HX[:, 0, k, :]), (lambda k: HX[:, 1, k, :])

                def tiles(slot, q, k):
                    for t in range(2):
                        ins = mm(AUX[:, t, slot * P:(slot + 1) * P], k[:, t * P:(t + 1) * P], q[:, t * P:(t + 1) * P],
                                 start=True, stop=True)
                    ins.then_inc(sc_mm, 1)

                def level(l):
                    pe.wait_ge(lv_mul, 9 * i + l + 1)
                    if l == 3:
                        pe.wait_ge(sc_read, 1 + 3 * i + 1)
                    tiles((l + 1) % 4, QL[:, l % 2, 0, :], QL[:, l % 2, 1, :])

                def between(l):
                    return lambda: level(l)

                prod("mix", i, 0, xh, xl, lambda k: ACC[:, 0, 0:T], between=None if peeled else lambda: mix_cross(i - 1))
                if not peeled:
                    mix_outputs(i - 1)
                pe.wait_ge(ks_ready, i + 1)
                pe.wait_ge(sc_read, 1 + 3 * i)
                tiles(0, QK1[:, 0, :], KS[:])
                level(0)
                mod_rest("mix", i, 1)
                prod("mix", i, 2, xh, xl, lambda k: ACC[:, 2, 0:T], between=between(1))
                if not peeled:
                    mix_turn(i - 1)
                level(2)
                mod_rest("mix", i, 3)
                prod("mix", i, 4, xh, xl, lambda k: ACC[:, 0, 0:T])
                level(3)
                level(4)
                mod_rest("mix", i, 5)
                prod("mix", i, 6, xh, xl, lambda k: ACC[:, 2, 0:T], between=between(5))
                level(6)
                mod_rest("mix", i, 7)

            mix_head(0, True)
            with pe.Fori(1, ITERS["mix"]) as i:
                mix_head(i, False)
            mix_cross(HEADS - 1)
            mix_outputs(HEADS - 1)
            mix_turn(HEADS - 1)

            pe.wait_ge(ya_ready, 1 + HEADS)
            pe.wait_ge(yb_ready, HEADS)
            with pe.Fori(0, ITERS["merge"]) as i:
                xh, xl = (lambda k: HX[:, 0, k, :]), (lambda k: HX[:, 1, k, :])
                for jj in range(2):
                    p = 4 * jj
                    prod("merge", i, p, xh, xl, lambda k: ACC[:, 0, 0:T])
                    prod("merge", i, p + 1, xh, xl, lambda k: ACC[:, 1, 0:T])
                    prod("merge", i, p + 2, lambda k: YAB[:, 2 * (k // 8), k % 8, :], lambda k: YAB[:, 2 * (k // 8) + 1, k % 8, :],
                         lambda k: ACC[:, 2, (k // 8) * T:(k // 8 + 1) * T], lambda k: (k % 8 == 0, k % 8 == 7))
                    mod_rest("merge", i, p + 3)

            pe.wait_ge(mrg_ready, KD)
            pe.wait_ge(zero_set, 1)
            mm(AUX[:, 0, 0:T], ONESR[:], ZERO[:], start=True, stop=False)
            with pe.Fori(0, ITERS["out"]) as i:
                def squares(n):
                    pe.wait_ge(sq2_done, 1 + 2 * i + n + 1)
                    mm(AUX[:, 0, 0:T], ONESR[:], SQ2[:, n % 2, :], start=False, stop=False).then_inc(ss2_mm, 1)

                for jj in range(2):
                    prod("out", i, 2 * jj, lambda k: MRG[:, 0, k, :], lambda k: MRG[:, 1, k, :], lambda k: ACC[:, 2 * jj, 0:T],
                         between=lambda: squares(jj - 1))
                    mod_rest("out", i, 2 * jj + 1)
            pe.wait_ge(sq2_done, 1 + KD)
            mm(AUX[:, 0, 0:T], ONESR[:], SQ2[:, 1, :], start=False, stop=True).then_inc(ss2_mm, 1)

            with pe.Fori(0, ITERS["up"]) as i:
                for p in range(4):
                    prod("up", i, p, lambda k: HX[:, 0, k, :], lambda k: HX[:, 1, k, :], lambda k: ACC[:, p, 0:T],
                         inputs=hx2_ready if p == 0 else None)

            pe.wait_ge(bank_free, UNIT0["down"] - 3)
            for n in range(2):
                mm(AUX[:, n, 0:T], ONESR[:], ZERO[:], start=True, stop=False)
            with pe.Fori(0, ITERS["down"]) as i:
                def squares(n):
                    pe.wait_ge(zero_set, 2)
                    pe.wait_ge(sq3_done, 1 + 2 * i + n + 1)
                    for m in range(2):
                        ins = mm(AUX[:, m, 0:T], ONESR[:], SQ3[:, n % 2, m, :], start=False, stop=False)
                    ins.then_inc(ss3_mm, 1)

                for jj in range(2):
                    for q in range(4):
                        p = 4 * jj + q
                        u = unit("down", i, p)[0]
                        if jj == 0:
                            pe.wait_ge(s_hidden, 1 + DT * (q + 1))
                        prod("down", i, p, lambda k: SH[:, DT * q + k, :], lambda k: SL[:, DT * q + k, :],
                             lambda k: ACC[:, jj, 0:T], lambda k: (q == 0 and k == 0, q == 3 and k == DT - 1),
                             bank_wait=u - 4 if q == 0 else False,
                             between=(lambda: squares(jj - 1)) if q == 1 else None)
            pe.wait_ge(sq3_done, 1 + KD)
            for m in range(2):
                ins = mm(AUX[:, m, 0:T], ONESR[:], SQ3[:, 1, m, :], start=False, stop=True)
            ins.then_inc(ss3_mm, 1)
            pe.wait_ge(sqm_done, 1)
            for k in range(KD):
                ins = mm(AUX[:, 2, 0:NMETA], ONESR[:], SQM[:, k, :], start=k == 0, stop=k == KD - 1)
            ins.then_inc(ssm_mm, 1)
            pe.wait_ge(lam_prod, 1)
            pe.wait_ge(at_const, 1)
            mm(AUX[:, 3, 0:2], ONEP[:], SMALL[:, 14:16], start=True, stop=True).then_inc(lam_mm, 1)
            pe.wait_ge(in_con2, 16)
            pe.wait_ge(lam_exp, 1)
            pe.wait_ge(rs4_done, 1)
            with pe.Fori(0, ITERS["attn"]) as i:
                def proj(p, meta, between=None, inputs=None):
                    a = 0 if meta else NMETA
                    prod("attn", i, p, lambda k: U2[:, 0, k, a:TA], lambda k: U2[:, 1, k, a:TA],
                         lambda k: ACC[:, p % 4, 0:TA - a], between=between, inputs=inputs)

                def tokens_major(src, bank):
                    for n, (a, w) in enumerate(((NMETA, P), (NMETA + P, P), (0, NMETA))):
                        ins = pe.transpose(AUX[0:w, bank, n * P:(n + 1) * P], src[:, a:a + w], c1("ident"))
                    return ins

                proj(0, False, inputs=u2_ready)
                proj(1, True)
                proj(2, True)
                pe.wait_ge(d_sq, i + 1)
                pe.wait_ge(mix_ready, 1 + 2 * i)
                mm(AUX[:, 0, 0:T], c2("blk64"), DR[:, 0, 0:T], start=True, stop=True)
                mm(AUX[:, 1, 0:TA], c2("blk64"), DR[:, 1, :], start=True, stop=True).then_inc(d_ms, 1)
                proj(3, False)
                pe.wait_ge(bank_free, unit("attn", i, 2)[0] + 1)
                tokens_major(DV, 2).then_inc(dv_tr, 1)
                pe.wait_ge(d_norm, i + 1)
                mm(AUX[:, 0, 0:T], c2("rot"), DN[:, 0, 0:T], start=True, stop=True)
                mm(AUX[:, 1, 0:TA], c2("rot"), DN[:, 1, :], start=True, stop=True).then_inc(d_rot, 1)
                proj(4, True)
                pe.wait_ge(d_rope, i + 1)
                for c in range(2):
                    r = slice(64 * c, 64 * c + 64)
                    mm(AUX[:, c, 0:P + NMETA], DQK[r, 0, 0:P], DQK[r, 1, 0:P + NMETA], start=True, stop=True)
                    ins = mm(AUX[:, c, P + NMETA:P + NMETA + TA], DQK[r, 0, P:T], DQK[r, 1, :], start=True, stop=True)
                ins.then_inc(d_sc, 1)
                proj(5, True)
                pe.wait_ge(d_max, i + 1)
                mm(AUX[:, 1, 0:T], SKF[:, NMETA:NMETA + P], SQF[:], start=True, stop=True)
                mm(AUX[:, 1, T:T + P], SKF[:, NMETA + P:TA], SQF[:, P:T], start=True, stop=True)
                pe.wait_ge(dvt_ready, i + 1)
                mm(AUX[0:NMETA, 2, 0:T], SKF[:, 0:NMETA], SQF[:], start=True, stop=True).then_inc(b_z, 1)

                def turns():
                    pe.wait_ge(d_w, i + 1)
                    q1 = P + NMETA
                    for n, a in enumerate((NMETA, q1 + NMETA, q1 + NMETA + P)):
                        pe.transpose(AUX[:, 3, n * P:(n + 1) * P], SS[:, 0, a:a + P], c1("ident"))
                    for n, a in enumerate((0, q1)):
                        ins = pe.transpose(AUX[0:NMETA, 0, n * P:(n + 1) * P], SS[:, 0, a:a + NMETA], c1("ident"))
                    ins.then_inc(d_wtr, 1)

                proj(6, False, turns)
                pe.wait_ge(d_wt, i + 1)
                mm(AUX[:, 0, 0:T], DVT[0:NMETA, 2, :], WTM[0:NMETA, :], start=True, stop=False)
                mm(AUX[:, 0, 0:T], DVT[:, 0, :], WTS[:, 0:T], start=False, stop=False)
                mm(AUX[:, 0, P:T], DVT[:, 1, :], WTS[:, T:T + P], start=False, stop=True).then_inc(d_av, 1)
                pe.wait_ge(bank_free, unit("attn", i, 5)[0] + 1)
                pe.wait_ge(b_zs, i + 1)
                tokens_major(SV, 2).then_inc(bv_tr, 1)
                pe.wait_ge(b_sp, i + 1)
                mm(AUX[:, 1, 0:T], c2("tri"), LZ[:, 0:T], start=True, stop=False)
                mm(AUX[:, 1, P:T], ONEP[:], LZ[:, T:T + P], start=False, stop=True)
                mm(AUX[:, 1, T:T + P], c2("tri"), LZ[:, T:T + P], start=True, stop=True)
                mm(AUX[0:NMETA, 3, 0:T], c2("tri")[0:NMETA, 0:NMETA], LM[0:NMETA, :], start=True, stop=False)
                mm(AUX[0:NMETA, 3, 0:T], ONEP[:, 0:NMETA], LZ[:, 0:T], start=False, stop=False)
                mm(AUX[0:NMETA, 3, P:T], ONEP[:, 0:NMETA], LZ[:, T:T + P], start=False, stop=True).then_inc(b_tail, 1)
                pe.wait_ge(d_osq, i + 1)
                pe.wait_ge(svt_ready, i + 1)
                mm(AUX[:, 2, 0:T], ON128[:], OD[:], start=True, stop=True).then_inc(d_oms, 1)
                proj(7, False)
                pe.wait_ge(b_a, i + 1)
                mm(AUX[:, 3, 0:T], SVT[0:NMETA, 2, :], AM[0:NMETA, :], start=True, stop=False)
                mm(AUX[:, 3, 0:T], SVT[:, 0, :], AZ[:, 0:T], start=False, stop=False)
                mm(AUX[:, 3, P:T], SVT[:, 1, :], AZ[:, T:T + P], start=False, stop=True).then_inc(b_av, 1)

            pe.wait_ge(mix_ready, 1 + 2 * HEADS)
            with pe.Fori(0, ITERS["proj"]) as i:
                for p in range(4):
                    prod("proj", i, p, lambda k: MIX[:, 0, k, :], lambda k: MIX[:, 1, k, :], lambda k: ACC[:, p, 0:T])

        @block.vector
        def _(dve):
            V = nc.vector
            for one in (vt_ready, sc_read, ya_ready, s_hidden, mix_ready):
                dve.sem_inc(one, 1)
            ch = Chain(dve, v_chain)
            link, mark = ch.link, ch.mark

            def lo(ph, i, p, only=(0, 1)):
                L = len(KINDS[ph])
                if p < L and KINDS[ph][p] == "m":
                    return
                s, slot = split(ph, i, p)
                for h in only:
                    a, b = (halves(ph) if p < L else ((0, 8), (8, 16)))[h]
                    dve.wait_ge(hi_half, 2 * s + h + 1)
                    V.tensor_tensor(LO[:, slot, a:b, :], RAW[:, p % 4, a:b, :], HI[:, slot, a:b, :].bitcast(F32),
                                    ALU.subtract).then_inc(lo_half, 1)

            def done(ph, i, p):
                dve.wait_ge(mm_half, 2 * unit(ph, i, p)[0] + 2)

            def modv(ph, i, p, idx):
                done(ph, i, p)
                V.tensor_scalar(MODV[:, bass.ds(idx, 1), 0:1].rearrange("p a b -> p (a b)"), ACC[:, p % 4, 0:1],
                                vcd("bmod", idx), None, ALU.add).then_inc(bank_free, 1)

            def split_small(dst_hi, dst_lo, src, ready=None):
                link(V.tensor_copy(dst_hi, src))
                ins = V.tensor_tensor(dst_lo, src, dst_hi.bitcast(F32), ALU.subtract)
                return ins

            V.memset(SMALL[:], 0.0)
            V.memset(ONESR[:], 1.0 / D)
            link(V.memset(ONE[:], 1.0))
            V.memset(SMALL[:, 0:1], EPS)
            V.memset(SMALL[:, 1:2], 1.0)
            V.memset(SMALL[:, 3:4], 1.0)
            V.memset(SMALL[:, 2:3], SUBLN_EPS).then_inc(ones_set, 1)
            dve.wait_ge(in_vec, 16)
            r0, r1 = vc("lb", 0, 16), vc("lb", 16, 16)
            link(V.tensor_tensor(LBV[:, 2, :], r0, r1, ALU.max))
            V.tensor_tensor(LBV[:, 0, :], r0, LBV[:, 2, :], ALU.subtract)
            V.tensor_tensor(LBV[:, 1, :], r1, LBV[:, 2, :], ALU.subtract).then_inc(lb_max, 1)
            dve.wait_ge(c_sig, 1)
            V.tensor_tensor(CS[:], CS[:], vc("c", 0, 2 * KD).rearrange("p (k s) -> p k s", s=2), ALU.mult).then_inc(c_silu, 1)
            dve.wait_ge(lb_exp, 1)
            link(V.tensor_tensor(LBV[:, 2, :], LBV[:, 0, :], LBV[:, 1, :], ALU.add))
            link(V.reciprocal(LBV[:, 2, :], LBV[:, 2, :]))
            link(V.tensor_tensor(LBV[:, 0, :], LBV[:, 0, :], LBV[:, 2, :], ALU.mult))
            link(V.tensor_scalar(LBV[:, 1, :], LBV[:, 0, :], -1.0, 1.0, ALU.mult, ALU.add))

            def rows(i, p):
                done("mod1", i, p)
                V.tensor_copy(ROW[0:2, p, :], ACC[0:2, p, 0:P]).then_inc(bank_free, 1)

            def mod1(i, peeled):
                for b in range(2):
                    j = 2 * i + b
                    for p in () if peeled else ((0, 1, 2), (3,))[b]:
                        rows(i, p)
                    dve.wait_ge(col_mm, 4 * i + 2 * b + 1)
                    V.tensor_scalar(MODV[:, bass.ds(j, 1), :].rearrange("p a b -> p (a b)"), AUX[:, 2 * b + 1, 0:2],
                                    vcd("bmod", j), None, ALU.add)
                    dve.wait_ge(col_mm, 4 * i + 2 * b + 2)
                    link(V.tensor_scalar(SMALL[:, 12:14], AUX[:, (2 * b + 2) % 4, 0:2], vcd("bmod", KD + j), 1.0,
                                         ALU.add, ALU.add))
                    am = AM1[:, bass.ds(j, 1), :].rearrange("p a s -> p (a s)")
                    link(V.tensor_scalar(am, SMALL[:, 12:14], vcd("norm1", j), None, ALU.mult))
                    dve.wait_ge(rs1_done, 1)
                    dve.wait_ge(h1_aff, 1 + j)
                    V.tensor_tensor(N1[:], XC[:, :, bass.ds(j, 1), :].rearrange("p s a t -> p s (a t)"), RS1[:],
                                    ALU.mult).then_inc(n1_ready, 1)
                    dve.wait_ge(h1_aff, 1 + j + 1)
                    hh = HX[:, 0:3:2, bass.ds(j, 1), :].rearrange("p s a t -> p s (a t)")
                    hl = HX[:, 1:4:2, bass.ds(j, 1), :].rearrange("p s a t -> p s (a t)")
                    link(V.tensor_copy(hh, HN1[:]))
                    V.tensor_tensor(hl, HN1[:], hh.bitcast(F32), ALU.subtract).then_inc(hx_ready, 1)

            for p in range(4):
                rows(0, p)
            for g in range(4):
                dve.wait_ge(sq1_done, g + 1)
                q = SQ1[:, g % 2]
                link(V.tensor_tensor(q[:, 0:2], q[:, 0:2], q[:, 2:4], ALU.add))
                ins = V.tensor_tensor(SS1[:] if g == 0 else q[:, 0], q[:, 0], q[:, 1], ALU.add)
                if g > 0:
                    link(ins)
                    ins = V.tensor_tensor(SS1[:], SS1[:], q[:, 0], ALU.add)
                ins.then_inc(sq1_read, 1)
                dve.wait_ge(sq1_read, g + 1)
            mod1(0, True)
            ch.straight()
            with dve.Fori(1, ITERS["mod1"]) as i:
                ch.enter(i - 1, CHAIN["v_mod1"])
                mod1(i, False)
            ch.leave(ITERS["mod1"] - 1, "v_mod1")
            lo("rec", 0, 0)

            with dve.Fori(0, ITERS["rec"]) as i:
                ch.enter(i, CHAIN["v_rec"])

                def head(t, d):
                    return t[:, d, bass.ds(i, 1), :].rearrange("p a t -> p (a t)")

                def gate(d):
                    dve.wait_ge(gate_sig, 3 * i + d + 1)
                    l0 = LBV[:, 0, bass.ds(HEADS * d + i, 1)]
                    l1 = LBV[:, 1, bass.ds(HEADS * d + i, 1)]
                    mark(V.tensor_scalar(head(FG, d), SG[:, d, 0, :], l1, l0, ALU.mult, ALU.add))
                    V.tensor_scalar(FC[:, d, :], SG[:, d, 1, :], l1, l0, ALU.mult, ALU.add).then_inc(bank_free, 1)

                lo("rec", i, 1)
                gate(0)
                lo("rec", i, 2)
                gate(1)
                ch.wait()
                dve.wait_ge(bank_free, unit("rec", i, 1)[0] + 1)
                link(V.tensor_scalar(LC[:], FC[:], TINY, None, ALU.max))
                V.tensor_scalar(FC[:], FC[:], -1.0, 1.0, ALU.mult, ALU.add).then_inc(ctx_f, 1)
                lo("rec", i, 3)
                dve.wait_ge(ctx_ln, i + 1)
                dve.wait_ge(kd_tr, 1 + i)
                V.memset(EXC[:, 0, T - 1:T], 0.0)
                mark(V.memset(EXC[:, 1, 0:1], 0.0))
                mark(V.tensor_tensor_scan(EXC[:, 0, 0:T - 1][:, ::-1], ONE[:, 0:T - 1], LC[:, 0, 1:T][:, ::-1], 0.0,
                                          ALU.mult, ALU.add))
                V.tensor_tensor_scan(EXC[:, 1, 1:T], ONE[:, 0:T - 1], LC[:, 1, 0:T - 1], 0.0,
                                     ALU.mult, ALU.add).then_inc(ctx_scan, 1)
                done("rec", i, 2)
                dve.wait_ge(v_tr, 1 + i)
                V.tensor_copy(VS[:].rearrange("p s t -> p (s t)"), ACC[:, 2, :]).then_inc(bank_free, 1)
                dve.wait_ge(ctx_exp, i + 1)
                dve.wait_ge(ctx_f, i + 1)
                V.tensor_tensor(EXC[:], EXC[:], FC[:], ALU.mult).then_inc(kd_ready, 1)
                dve.wait_ge(v_tr, 1 + i + 1)
                dve.wait_ge(s_mm, 1 + i)
                mark(V.tensor_copy(VCT[:].rearrange("p t d -> p (t d)"), AUX[:, 1, T:2 * T]))
                V.tensor_copy(VT[:, :, bass.ds(i * P, P)], AUX[:, 1, 0:T].rearrange("p (t d) -> p t d", t=2)).then_inc(vt_ready, 1)
                lo("rec", i, 4)
                dve.wait_ge(gate_sig, 3 * i + 3)
                V.tensor_tensor(QF[:, bass.ds(i, 1), :].rearrange("p a t -> p (a t)"), ACC[:, 3, 0:T], SGQ[:],
                                ALU.mult).then_inc(bank_free, 1)
            ch.leave(ITERS["rec"], "v_rec")

            GSIG = 3 * HEADS
            link(V.memset(UP[:], 0.0))
            ch.straight()
            dve.wait_ge(vt_ready, 1 + HEADS)
            dve.wait_ge(s_mm, 1 + HEADS)
            dve.wait_ge(bank_free, UNIT0["mix"])

            def mix_on(i):
                dve.wait_ge(o_rstd, i + 1)
                mark(V.tensor_scalar(ON[:, 0, :], AUX[:, 3, 0:P], SMALL[:, 10:11], None, ALU.mult))
                V.tensor_scalar(ON[:, 1, :], AUX[:, 3, P:T], SMALL[:, 11:12], None, ALU.mult).then_inc(on_ready, 1)

            def mix_ya(i):
                x = lambda d: YAB[:, d, bass.ds(i, 1), :].rearrange("p a t -> p (a t)")
                dve.wait_ge(on_tr, i + 1)
                link(V.scalar_tensor_tensor(YT[:], AUX[:, 2, T:2 * T], vc("anorm"), GS[:], ALU.mult, ALU.mult))
                split_small(x(0), x(1), YT[:]).then_inc(ya_ready, 1)

            def mix_head(i, peeled):

                def totals(l, n):
                    return (TT0, TT1)[l % 2][:, :, 0:n]

                def level(l):
                    h = 1 << l
                    nb = T // (2 * h)
                    dve.wait_ge(lv_exp, 1 + 9 * i + l + 1)
                    q = QL[:, l % 2].rearrange("p a (n two h) -> p a n two h", two=2, h=h)
                    for side, src in ((1, QK1), (0, QK0)):
                        o = src[:].rearrange("p a (n two h) -> p a n two h", two=2, h=h)
                        ins = V.tensor_tensor(q[:, :, :, side, :], q[:, :, :, side, :], o[:, :, :, side, :], ALU.mult)
                    ins.then_inc(lv_mul, 1)
                    ch.wait()
                    dve.wait_ge(lv_sum, 9 * i + l + 1)
                    r = AR[:].rearrange("p a (n two h) -> p a n two h", two=2, h=h)
                    tt = totals(l, 2 * nb).rearrange("p a (n two) -> p a n two", two=2)
                    right, left = r[:, 0:2, :, 1, :], r[:, 2:4, :, 0, :]
                    if l < LEVELS - 1:
                        mark(V.tensor_tensor(totals(l + 1, nb), tt[:, :, :, 0], tt[:, :, :, 1], ALU.add))
                    mark(V.tensor_tensor(right, right, tt[:, 0:2, :, 0].unsqueeze(3).broadcast_to([P, 2, nb, h]), ALU.add))
                    V.tensor_tensor(left, left, tt[:, 1:3, :, 1].unsqueeze(3).broadcast_to([P, 2, nb, h]),
                                    ALU.add).then_inc(lv_sum, 1)

                def mask(g, out):
                    dve.wait_ge(sc_mm, 1 + 9 * i + 4 * g + 4)
                    m = c1("masks")[:, 4 * g * P:4 * (g + 1) * P].unsqueeze(1).broadcast_to([P, 2, 4 * P])
                    V.tensor_tensor(SCT[:].rearrange("p t s n -> p t (s n)"), AUX[:, 0:2, :], m, ALU.mult).then_inc(sc_read, 1)
                    dve.wait_ge(sc_read, 1 + 3 * i + g + 1)
                    for t in range(2):
                        ins = V.tensor_reduce(out(t), SCT[:, t].rearrange("p s n -> p n s"), AX.X, ALU.add)
                        mark(ins)
                    ch.wait()

                x = lambda t, d: t[:, d, bass.ds(i, 1), :].rearrange("p a t -> p (a t)")
                qf = QF[:, bass.ds(i, 1), :].rearrange("p a t -> p (a t)")
                V.tensor_scalar(TT0[:, 0:2, :], FG[:, :, bass.ds(i, 1), :].rearrange("p d a t -> p d (a t)"), TINY, None,
                                ALU.max).then_inc(f_ready, 1)
                dve.wait_ge(sc_mm, 1 + 9 * i)
                mark(V.tensor_scalar(QK0[:, 1, :], x(FG, 0), -1.0, 1.0, ALU.mult, ALU.add))
                mark(V.tensor_scalar(QK1[:, 1, :], x(FG, 1), -1.0, 1.0, ALU.mult, ALU.add))
                mark(V.tensor_copy(QK0[:, 0, :], qf))
                mark(V.tensor_copy(QK1[:, 0, :], qf))
                ch.wait()
                V.tensor_tensor(KS[:], QK0[:, 1, :], QK1[:, 1, :], ALU.add).then_inc(ks_ready, 1)
                dve.wait_ge(lv_exp, 1 + 9 * i)
                mark(V.memset(AR[:, 1, :], 0.0))
                mark(V.memset(AR[:, 3, :], 0.0))
                dve.wait_ge(f_ln, i + 1)
                mark(V.tensor_copy(TT0[:, 0:2, :], AR[:, 0:3:2, :]))
                V.tensor_copy(TT0[:, 2, :], AR[:, 0, :]).then_inc(lv_sum, 1)
                level(0)
                lo("mix", i, 2)
                level(1)
                if not peeled:
                    mix_on(i - 1)
                level(2)
                lo("mix", i, 4)
                if not peeled:
                    mix_ya(i - 1)
                    dve.wait_ge(ya_ready, 1 + i)
                dve.wait_ge(gate_sig, GSIG + i + 1)
                V.tensor_tensor(GS[:], ACC[:, 0, 0:T], SGG[:], ALU.mult).then_inc(bank_free, 1)
                modv("mix", i, 1, 48 + 4 * i)
                done("mix", i, 2)
                V.tensor_copy(SCB[:], ACC[:, 2, 0:T]).then_inc(bank_free, 1)
                level(3)
                modv("mix", i, 3, 49 + 4 * i)
                dve.wait_ge(o_mm, 1 + i)
                mask(0, lambda t: SC[:, t, t * P:(t + 1) * P])
                lo("mix", i, 6)
                level(4)
                done("mix", i, 4)
                V.tensor_tensor(UP[:, 1:T + 1], ACC[:, 0, 0:T], SCB[:], ALU.mult).then_inc(bank_free, 1)
                dve.wait_ge(bank_free, unit("mix", i, 4)[0] + 1)
                w = lambda n: vcd("sconv", HEADS * n + i)
                link(V.tensor_scalar(SGG[:], UP[:, 1:T + 1], w(1), None, ALU.mult))
                link(V.scalar_tensor_tensor(SGG[:], UP[:, 0:T], w(0), SGG[:], ALU.mult, ALU.add))
                link(V.scalar_tensor_tensor(SGG[:], UP[:, 2:T + 2], w(2), SGG[:], ALU.mult, ALU.add))
                modv("mix", i, 5, 50 + 4 * i)
                level(5)
                lo("mix", i, 8)
                level(6)
                done("mix", i, 6)
                V.tensor_tensor(SCB[:], ACC[:, 2, 0:T], SGG[:], ALU.mult).then_inc(bank_free, 1)
                dve.wait_ge(bank_free, unit("mix", i, 6)[0] + 1)
                split_small(x(YAB, 2), x(YAB, 3), SCB[:]).then_inc(yb_ready, 1)
                level(7)
                modv("mix", i, 7, 51 + 4 * i)
                dve.wait_ge(lv_exp, 1 + 9 * i + 9)
                V.tensor_tensor(QS[:], QS[:], qf.unsqueeze(1).broadcast_to([P, 2, T]), ALU.mult).then_inc(lv_mul, 1)
                mask(1, lambda t: KS[:, t * P:(t + 1) * P])
                for t in range(2):
                    d = SC[:, t, t * P:(t + 1) * P]
                    mark(V.tensor_tensor(d, d, KS[:, t * P:(t + 1) * P], ALU.add))
                dve.wait_ge(sc_mm, 1 + 9 * i + 9)
                mark(V.tensor_copy(SC[:, 0, P:T], AUX[:, 2, 0:P]))
                V.tensor_copy(SC[:, 1, 0:P], AUX[:, 2, P:T]).then_inc(sc_read, 1)

            mix_head(0, True)
            ch.straight()
            with dve.Fori(1, ITERS["mix"]) as i:
                ch.enter(i - 1, CHAIN["v_mix"])
                mix_head(i, False)
            ch.leave(ITERS["mix"] - 1, "v_mix")
            mix_on(HEADS - 1)
            mix_ya(HEADS - 1)
            ch.straight()
            GSIG += HEADS

            dve.wait_ge(ya_ready, 1 + HEADS)
            with dve.Fori(0, ITERS["merge"]) as i:
                ch.enter(i, CHAIN["v_merge"])
                for jj in range(2):
                    p, j = 4 * jj, 2 * i + jj
                    lo("merge", i, p + 1)
                    lo("merge", i, p + 2)
                    lo("merge", i, p + 4)
                    done("merge", i, p + 2)
                    dve.wait_ge(gate_sig, GSIG + 2 * j + 2)
                    V.tensor_tensor(M1[:], ACC[:, 2, 0:T], GA[:], ALU.mult).then_inc(bank_free, 1)
                    V.tensor_tensor(M2[:], ACC[:, 2, T:2 * T], GB[:], ALU.mult).then_inc(bank_free, 1)
                    dve.wait_ge(bank_free, unit("merge", i, p + 2)[0])
                    V.tensor_tensor(M1[:], M1[:], M2[:], ALU.add).then_inc(bank_free, 1)
                    dve.wait_ge(bank_free, unit("merge", i, p + 2)[0] + 1)
                    o = lambda s: MRG[:, s, bass.ds(j, 1), :].rearrange("p a t -> p (a t)")
                    link(V.tensor_copy(o(0), M1[:]))
                    V.tensor_tensor(o(1), M1[:], o(0).bitcast(F32), ALU.subtract).then_inc(mrg_ready, 1)
                    modv("merge", i, p + 3, 32 + j)
            ch.leave(ITERS["merge"], "v_merge")
            GSIG += 2 * KD

            dve.wait_ge(mrg_ready, KD)
            V.memset(SQ2[:, 1, :], 0.0)
            V.memset(ZERO[:], 0.0).then_inc(zero_set, 1)
            dve.wait_ge(in_x1, 16)
            with dve.Fori(0, ITERS["out"]) as i:
                ch.enter(i, CHAIN["v_out"])
                for jj in range(2):
                    j = 2 * i + jj
                    if jj == 1:
                        dve.wait_ge(raw_full[3], 16 * (unit("out", i, 3)[1] + 1))
                        w = RAW[:, 3]
                        for k in range(KD):
                            if k >= 2:
                                ch.wait_but_last()
                            if k < 2:
                                ins = V.tensor_scalar(w[:, k, :], w[:, k, :], CS[:, k, 0:1], None, ALU.mult)
                            else:
                                ins = V.scalar_tensor_tensor(w[:, k % 2, :], w[:, k, :], CS[:, k, 0:1], w[:, k % 2, :],
                                                             ALU.mult, ALU.add)
                            if k < KD - 1:
                                mark(ins)
                        ins.then_inc(mod_sum_v, 1)
                    lo("out", i, 2 * jj + 2)
                    done("out", i, 2 * jj)
                    x1 = X1[:, bass.ds(j, 1), :].rearrange("p a t -> p (a t)")
                    g1 = MODV[:, bass.ds(32 + j, 1), 0:1].rearrange("p a b -> p (a b)")
                    V.scalar_tensor_tensor(x1, ACC[:, 2 * jj, 0:T], g1, x1, ALU.mult, ALU.add).then_inc(bank_free, 1)
                    modv("out", i, 2 * jj + 1, 80 + j)
            ch.leave(ITERS["out"], "v_out")
            dve.wait_ge(bank_free, UNIT0["up"])
            link(V.scalar_tensor_tensor(AM2[:], MODV[:, 64:80, 0], 1.0, vc("norm2", 0, KD), ALU.add, ALU.mult))
            dve.wait_ge(rs2_done, 1)
            for g in range(5):
                if g < 4:
                    V.tensor_tensor(N2[:, 4 * (g % 2):4 * (g % 2) + 4, :], X1[:, 4 * g:4 * g + 4, :],
                                    RS2[:].unsqueeze(1).broadcast_to([P, 4, T]), ALU.mult).then_inc(n2_ready, 1)
                if g > 0:
                    n = N2[:, 4 * ((g - 1) % 2):4 * ((g - 1) % 2) + 4, :]
                    dve.wait_ge(h2_aff, g)
                    split_small(HX[:, 0, 4 * g - 4:4 * g, :], HX[:, 1, 4 * g - 4:4 * g, :], n).then_inc(hx2_ready, 1)
                    dve.wait_ge(hx2_ready, g)
            ch.straight()

            dve.wait_ge(x1_out, 16)
            V.memset(AT[:], 0.0).then_inc(cv_ready, 1)
            with dve.Fori(0, ITERS["up"]) as i:
                ch.enter(i, CHAIN["v_up"])
                for jj in range(2):
                    j = 2 * i + jj

                    def tap(r, c):
                        return AT[:, r:r + 4, c:c + GRID], vcd("dw", FF * (3 * r + c) + j)

                    lo("up", i, 2 * jj + 1)
                    dve.wait_ge(s_hidden, 1 + j)
                    taps = [(r, c) for r in range(3) for c in range(3) if (r, c) != (1, 1)]
                    acc4 = [t[:].rearrange("p (r c) -> p r c", c=GRID) for t in (CV2, CV)]
                    dve.wait_ge(a_copied, j + 1)
                    a, w = tap(*taps[0])
                    V.tensor_scalar(acc4[0], a, w, None, ALU.mult).then_inc(bank_free, 1)
                    for n, rc in enumerate(taps[1:], 1):
                        a, w = tap(*rc)
                        if n == 4:
                            lo("up", i, 2 * jj + 2, (0,))
                        if n == 2:
                            dve.wait_ge(bank_free, unit("up", i, 2 * jj)[0] + 1)
                        elif n > 2:
                            ch.wait_but_last()
                        mark(V.scalar_tensor_tensor(acc4[n % 2], a, w, acc4[n % 2], ALU.mult, ALU.add))
                    ch.wait()
                    V.tensor_tensor(CV[:], CV[:], CV2[:], ALU.add).then_inc(cv_ready, 1)
                    lo("up", i, 2 * jj + 2, (1,))
                    dve.wait_ge(cv_sig, 1 + j + 1)
                    done("up", i, 2 * jj + 1)
                    V.tensor_tensor(CV2[:], ACC[:, 2 * jj + 1, 0:T], S1[:], ALU.mult).then_inc(bank_free, 1)
                    dve.wait_ge(bank_free, unit("up", i, 2 * jj + 1)[0] + 1)
                    o = lambda t: t[:, bass.ds(j, 1), :].rearrange("p a t -> p (a t)")
                    split_small(o(SH), o(SL), CV2[:]).then_inc(s_hidden, 1)
            ch.leave(ITERS["up"], "v_up")

            dve.wait_ge(cv_sig, 1 + FF)
            dve.wait_ge(s_hidden, 1 + FF)
            V.memset(SQ3[:, 1], 0.0).then_inc(zero_set, 1)
            dve.wait_ge(in_x1b, 16)
            with dve.Fori(0, ITERS["down"]) as i:
                for jj in range(2):
                    j = 2 * i + jj
                    for q in range(4):
                        lo("down", i, 4 * jj + q + 1)
                    done("down", i, 4 * jj + 3)
                    xf = XF[:, bass.ds(j, 1), :].rearrange("p a t -> p (a t)")
                    g2 = MODV[:, bass.ds(80 + j, 1), 0:1].rearrange("p a b -> p (a b)")
                    V.scalar_tensor_tensor(xf, ACC[:, jj, 0:T], g2, xf, ALU.mult, ALU.add).then_inc(bank_free, 4)
            dve.wait_ge(bank_free, UNIT0["attn"])
            V.memset(ONEP[:], 1.0)
            V.memset(ON128[:], 1.0 / P).then_inc(at_const, 1)
            o = VCOLS["lam"][0]
            V.tensor_tensor(SMALL[:, 14:16], VEC[:, o:o + 2], VEC[:, o + 2:o + 4], ALU.mult).then_inc(lam_prod, 1)
            mark(V.tensor_scalar(SMALL[:, 20:21], vc("subln"), 1.0 - LAM_INIT, None, ALU.mult))
            dve.wait_ge(rs3_done, 1)
            link(V.tensor_tensor(MSF[:], RSF[:], RSF[:], ALU.mult))
            V.tensor_tensor(MSF[:], MSF[:], AUX[:, 1, 0:T], ALU.mult).then_inc(ms4_done, 1)
            for k in range(KD):
                V.scalar_tensor_tensor(XF[:, k, :], XF[:, k, :], vc("final", k), RSF[:], ALU.mult, ALU.mult).then_inc(xf_ready, 1)
            dve.wait_ge(xf_ready, KD)
            dve.wait_ge(in_meta, 16)
            dve.wait_ge(rs4_done, 1)
            for g in range(4):
                for k in range(4 * g, 4 * g + 4):
                    mark(V.scalar_tensor_tensor(N3[:, k % 4, 0:NMETA], METT[:, k, :], vc("norm_2", k), RS3[:, 0:NMETA],
                                                ALU.mult, ALU.mult))
                    mark(V.scalar_tensor_tensor(N3[:, k % 4, NMETA:TA], XF[:, k, :], vc("norm_2", k), RS3[:, NMETA:TA],
                                                ALU.mult, ALU.mult))
                ch.wait()
                split_small(U2[:, 0, 4 * g:4 * g + 4, :], U2[:, 1, 4 * g:4 * g + 4, :], N3[:]).then_inc(u2_ready, 1)
                dve.wait_ge(u2_ready, g + 1)
            dve.wait_ge(lam_exp, 1)
            link(V.tensor_tensor(SMALL[:, 18:19], SMALL[:, 16:17], SMALL[:, 17:18], ALU.subtract))
            link(V.tensor_scalar(SMALL[:, 19:20], SMALL[:, 18:19], LAM_INIT, None, ALU.add))
            ch.straight()

            dve.wait_ge(in_con2, 16)
            sc = float(P) ** -0.5
            q1 = P + NMETA
            with dve.Fori(0, ITERS["attn"]) as i:
                ch.enter(i, CHAIN["v_attn"])

                def take(p, dst, n):
                    done("attn", i, p)
                    V.tensor_copy(dst, ACC[:, p % 4, 0:n]).then_inc(bank_free, 1)

                def mixed(g):
                    o = lambda s: MIX[:, s, bass.ds(HEADS * g + i, 1), :].rearrange("p a t -> p (a t)")
                    split_small(o(0), o(1), MT[:]).then_inc(mix_ready, 1)

                lo("attn", i, 1)
                dve.wait_ge(d_sc, 1 + i)
                take(0, DQK[:, 0, 0:T], T)
                lo("attn", i, 2)
                take(1, DQK[:, 1, :], TA)
                dve.wait_ge(bank_free, unit("attn", i, 1)[0] + 1)
                mark(V.tensor_tensor(DR[:, 0, 0:T], DQK[:, 0, 0:T], DQK[:, 0, 0:T], ALU.mult))
                V.tensor_tensor(DR[:, 1, :], DQK[:, 1, :], DQK[:, 1, :], ALU.mult).then_inc(d_sq, 1)
                lo("attn", i, 3)
                dve.wait_ge(dv_tr, 1 + i)
                take(2, DV[:], TA)
                dve.wait_ge(d_rstd, i + 1)
                mark(V.scalar_tensor_tensor(DN[:, 0, 0:T], DQK[:, 0, 0:T], vc("qn"), DR[:, 0, 0:T], ALU.mult, ALU.mult))
                V.scalar_tensor_tensor(DN[:, 1, :], DQK[:, 1, :], vc("kn"), DR[:, 1, :], ALU.mult, ALU.mult).then_inc(d_norm, 1)
                lo("attn", i, 4)
                dve.wait_ge(dv_tr, 1 + i + 1)
                dve.wait_ge(d_av, 1 + i)
                mark(V.tensor_copy(DVT[:, 0:2, :].rearrange("p a d -> p (a d)"), AUX[:, 2, 0:T]))
                V.tensor_copy(DVT[0:NMETA, 2, :], AUX[0:NMETA, 2, T:T + P]).then_inc(dvt_ready, 1)
                ch.wait()
                dve.wait_ge(d_norm, i + 1)
                mark(V.tensor_tensor(DR[:, 0, 0:T], DN[:, 0, 0:T], c2("cos")[:, NMETA:TA], ALU.mult))
                mark(V.tensor_tensor(DR[:, 1, :], DN[:, 1, :], c2("cos"), ALU.mult))
                dve.wait_ge(d_rot, i + 1)
                mark(V.tensor_tensor(DQK[:, 0, 0:T], AUX[:, 0, 0:T], c2("sin")[:, NMETA:TA], ALU.mult))
                mark(V.tensor_tensor(DQK[:, 1, :], AUX[:, 1, 0:TA], c2("sin"), ALU.mult))
                ch.wait()
                mark(V.tensor_tensor(DQK[:, 0, 0:T], DQK[:, 0, 0:T], DR[:, 0, 0:T], ALU.add))
                V.tensor_tensor(DQK[:, 1, :], DQK[:, 1, :], DR[:, 1, :], ALU.add).then_inc(d_rope, 1)
                dve.wait_ge(b_z, 1 + i)
                take(3, SQF[:], T)
                lo("attn", i, 5)
                take(4, SKF[:], TA)
                dve.wait_ge(d_sc, 1 + i + 1)
                link(V.scalar_tensor_tensor(SS[:], AUX[:, 0:2, 0:q1 + TA], 0.125,
                                            c2("dfmask").unsqueeze(1).broadcast_to([P, 2, q1 + TA]), ALU.mult, ALU.add))
                mark(V.tensor_reduce(ATS[:, 12:14], SS[:, :, 0:q1], AX.X, ALU.max))
                link(V.tensor_reduce(ATS[:, 14:16], SS[:, :, q1:q1 + TA], AX.X, ALU.max))
                V.tensor_scalar(ATS[:, 0:4], ATS[:, 12:16], -1.0, None, ALU.mult).then_inc(d_max, 1)
                lo("attn", i, 6)
                dve.wait_ge(d_exp, i + 1)
                link(V.reciprocal(ATS[:, 8:12], ATS[:, 4:8]))
                for t in range(2):
                    mark(V.tensor_scalar(ATS[:, 16 + t:17 + t], ATS[:, 9 + 2 * t:10 + 2 * t], SMALL[:, 19:20], None, ALU.mult))
                ch.wait()
                for t, r in enumerate((slice(0, q1), slice(q1, q1 + TA))):
                    mark(V.tensor_scalar(SS[:, 1, r], SS[:, 1, r], ATS[:, 16 + t:17 + t], None, ALU.mult))
                ch.wait()
                for t, r in enumerate((slice(0, q1), slice(q1, q1 + TA))):
                    ins = V.scalar_tensor_tensor(SS[:, 0, r], SS[:, 0, r], ATS[:, 8 + 2 * t:9 + 2 * t], SS[:, 1, r],
                                                 ALU.mult, ALU.subtract)
                ins.then_inc(d_w, 1)
                dve.wait_ge(b_z, 1 + i + 1)
                mark(V.scalar_tensor_tensor(ZS[:], AUX[:, 1, 0:3 * P], sc, c2("sbmask"), ALU.mult, ALU.add))
                V.tensor_scalar(ZM[0:NMETA, :], AUX[0:NMETA, 2, 0:T], sc, None, ALU.mult).then_inc(b_zs, 1)
                dve.wait_ge(bv_tr, 1 + i)
                take(5, SV[:], TA)
                dve.wait_ge(d_wtr, i + 1)
                mark(V.tensor_copy(WTS[:], AUX[:, 3, 0:3 * P]))
                V.tensor_copy(WTM[0:NMETA, :], AUX[0:NMETA, 0, 0:T]).then_inc(d_wt, 1)
                lo("attn", i, 7)
                dve.wait_ge(b_ln, i + 1)
                ch.wait()
                dve.wait_ge(b_zs, i + 1)
                mark(V.scalar_tensor_tensor(LZ[:], ZS[:], 0.0, LZ[:], ALU.max, ALU.add))
                V.scalar_tensor_tensor(LM[0:NMETA, :], ZM[0:NMETA, :], 0.0, LM[0:NMETA, :], ALU.max, ALU.add).then_inc(b_sp, 1)
                dve.wait_ge(bv_tr, 1 + i + 1)
                dve.wait_ge(b_av, 1 + i)
                mark(V.tensor_copy(SVT[:, 0:2, :].rearrange("p a d -> p (a d)"), AUX[:, 2, 0:T]))
                V.tensor_copy(SVT[0:NMETA, 2, :], AUX[0:NMETA, 2, T:T + P]).then_inc(svt_ready, 1)
                dve.wait_ge(b_tail, i + 1)
                mark(V.tensor_tensor(AZ[:], ZS[:], AUX[:, 1, 0:3 * P], ALU.subtract))
                V.tensor_tensor(AM[0:NMETA, :], ZM[0:NMETA, :], AUX[0:NMETA, 3, 0:T], ALU.subtract).then_inc(b_arg, 1)
                lo("attn", i, 8)
                dve.wait_ge(d_orstd, i + 1)
                link(V.scalar_tensor_tensor(MT[:], AUX[:, 0, 0:T], SMALL[:, 20:21], RSD[:], ALU.mult, ALU.mult))
                dve.wait_ge(gate_sig, GSIG + 2 * i + 2)
                V.tensor_tensor(GSB[:], ACC[:, 2, 0:T], GSB[:], ALU.mult).then_inc(bank_free, 1)
                V.tensor_tensor(GDF[:], ACC[:, 3, 0:T], GDF[:], ALU.mult).then_inc(bank_free, 1)
                dve.wait_ge(bank_free, unit("attn", i, 8)[0])
                link(V.tensor_tensor(MT[:], MT[:], GDF[:], ALU.mult))
                mixed(1)
                dve.wait_ge(mix_ready, 1 + 2 * i + 1)
                dve.wait_ge(b_av, 1 + i + 1)
                link(V.tensor_tensor(MT[:], AUX[:, 3, 0:T], GSB[:], ALU.mult))
                mixed(0)
            ch.leave(ITERS["attn"], "v_attn")

            def put(i, p):
                done("proj", i, p)
                V.tensor_tensor(OUTS[:, bass.ds(4 * i + p, 1), :].rearrange("p a t -> p (a t)"), ACC[:, p, 0:T], XF[:, bass.ds(4 * i + p, 1), :].rearrange("p a t -> p (a t)"),
                                ALU.add).then_inc(bank_free, 1)

            dve.wait_ge(mix_ready, 1 + 2 * HEADS)
            with dve.Fori(0, ITERS["proj"] - 1) as i:
                for p in range(4):
                    lo("proj", i, p + 1)
                    put(i, p)
            for p in range(4):
                if p < 3:
                    lo("proj", ITERS["proj"] - 1, p + 1)
                put(ITERS["proj"] - 1, p)


def constants():
    n = np.arange(P)
    masks = [np.eye(P)]
    for l in range(LEVELS - 1):
        masks.append((n[:, None] >> (l + 1) == n[None, :] >> (l + 1)) & ((n[:, None] >> l) != (n[None, :] >> l)))
    con1 = np.concatenate([np.eye(P)] + masks, axis=1).astype(np.float32)
    tri = n[:, None] >= n[None, :]
    rot, half = np.zeros((P, P)), 8
    cos, sin = np.ones((P, TA), np.float32), np.zeros((P, TA), np.float32)
    inv = (np.float32(500000.0) ** (-np.arange(0, 2 * half, 2, dtype=np.float32) / np.float32(2 * half))).astype(np.float32)
    ang = (np.arange(TA, dtype=np.float32)[None, :] * inv[:, None]).astype(np.float32)
    for g in (0, 64):
        for d in range(half):
            rot[g + half + d, g + d] = -1.0
            rot[g + d, g + half + d] = 1.0
            for o in (d, half + d):
                cos[g + o], sin[g + o] = np.cos(ang[d]), np.sin(ang[d])
    strict = np.where(n[:, None] < n[None, :], 0.0, NEG)
    sbmask = np.concatenate([strict, np.zeros((P, P)), strict], axis=1)
    pos = np.arange(TA)
    df = [np.where(pos[None, :P + NMETA] <= n[:, None] + NMETA, 0.0, NEG),
          np.where(pos[None, :] <= n[:, None] + NMETA + P, 0.0, NEG)]
    blk = np.kron(np.eye(2), np.full((64, 64), 1.0 / 64))
    con2 = np.concatenate([tri, rot, cos, sin, sbmask] + df + [blk], axis=1).astype(np.float32)
    return con1, con2


def kernel(**inputs):
    import numpy as np
    import concourse.bacc as bacc
    from concourse.bass_utils import run_bass_kernel_spmd

    g = {k: np.asarray(v) for k, v in inputs.items()}

    def blocks(v):
        return np.ascontiguousarray(v.reshape(-1, P).T)

    def units(w):
        k, n = w.shape
        return w.reshape(k // P, P, n // P, P).transpose(2, 1, 0, 3)

    wm, wi = units(g["w_mod"][0]), units(g["w_in"][0])
    pab = np.concatenate([units(g["w_pa"][0]), units(g["w_pb"][0])], axis=2)
    wo, wu = units(g["w_o"][0]), units(g["w_up"][0])
    w2, wo2 = units(g["w_in_2"][0]), units(g["w_out_2"][0])
    order = []
    for j in range(KD):
        order += [wm[j], wm[KD + j]]
    for h in range(HEADS):
        order += [wi[8 + h], wi[16 + h], wi[24 + h], wi[h]]
    for h in range(HEADS):
        for n, b in enumerate((32, 48, 56, 40)):
            order += [wi[b + h], wm[48 + 4 * h + n]]
    for j in range(KD):
        order += [wi[64 + j], wi[80 + j], pab[j], wm[32 + j]]
    for j in range(KD):
        order += [wo[j], wm[80 + j]]
    for j in range(FF):
        order += [wu[j], wu[FF + j]]
    for h in range(HEADS):
        order += [w2[b + h] for b in (32, 40, 48, 0, 8, 16, 24, 56)]
    order += [wo2[j] for j in range(KD)]
    wts = np.stack(order)
    wd = g["w_down"][0].reshape(4, DT, P, KD, P).transpose(3, 0, 2, 1, 4).reshape(4 * KD, P, DT, P)
    lam = np.zeros((P, 4), np.float32)
    for n, name in enumerate(("lambda_q1_2", "lambda_q2_2", "lambda_k1_2", "lambda_k2_2")):
        lam[:64, n] = g[name][0]
    vec = np.concatenate([
        blocks(g["norm1_g"][0]), blocks(g["norm2_g"][0]), blocks(g["final_g"]), blocks(g["norm_w_2"][0]),
        blocks(g["b_mod"][0]), blocks(g["lb_raw"].reshape(-1)), blocks(g["a_norm_g"][0]),
        blocks(g["sconv_w"][0].reshape(-1)), blocks(g["ffn_dw"][0].reshape(-1)), blocks(g["ffn_db"][0]),
        blocks(np.tile(g["q_norm_w_2"][0], 2)), blocks(np.tile(g["k_norm_w_2"][0], 2)), blocks(g["subln_w_2"][0]),
        np.stack([blocks(g["c"][0]), blocks(g["c_ctx"])], axis=2).reshape(P, -1), lam], axis=1)
    con1, con2 = constants()
    arrays = {
        "xct": np.stack([g["x"][0].T, g["ctx"][0].T]), "metat": np.ascontiguousarray(g["meta_2"].T), "vec": vec,
        "con1": con1, "con2": con2, "wts": wts, "wdown": np.ascontiguousarray(wd),
    }
    nc = bacc.Bacc("TRN2", target_bir_lowering=False, num_devices=1)
    args = [nc.dram_tensor(n, a.shape, F32, kind="ExternalInput").ap() for n, a in arrays.items()]
    args.append(nc.dram_tensor("park", (P, KD, T), F32, kind="Internal").ap())
    args.append(nc.dram_tensor("outt", (KD, P, T), F32, kind="ExternalOutput").ap())
    build(nc, *args)
    r = run_bass_kernel_spmd(nc, [arrays], core_ids=[0])
    return np.ascontiguousarray(r.results[0]["outt"].reshape(D, T).T)[None]
```
